# Optimizing a Trainium2 kernel written in Bass

```python
import math
import jax
import jax.numpy as jnp
from jax import lax
import numpy as np

D_MODEL = 2048
BATCH = 1
SEQ = 256
DEPTH = 1

CHUNK = 64
NORM_EPS = 1e-6
RWKV_HEAD_DIM = 64
RWKV_HEADS = D_MODEL // RWKV_HEAD_DIM
RWKV_DECAY_LORA = 96
RWKV_AAA_LORA = 96
RWKV_GATE_LORA = 256
RWKV_GN_EPS = 64e-5
GDN_HEAD_DIM = 128
GDN_HEADS = D_MODEL // GDN_HEAD_DIM
GDN_CONV = 4
D_FF = -(-8 * D_MODEL // (3 * 256)) * 256

RWKV_SPLITS = (D_MODEL, D_MODEL, D_MODEL, RWKV_DECAY_LORA, RWKV_AAA_LORA, RWKV_GATE_LORA)
RWKV_COLS = sum(RWKV_SPLITS)
IN_SPLITS = (RWKV_COLS, 3 * D_MODEL, D_MODEL, GDN_HEADS, GDN_HEADS, D_MODEL, D_MODEL)
IN_COLS = sum(IN_SPLITS)

kernel_name = 'hybrid_rwkv7_gdn_sandwich_block'

def _split(t, sizes):
    return jnp.split(t, [int(s) for s in np.cumsum(sizes)[:-1]], axis=-1)

def rmsnorm(x, w, eps=NORM_EPS):
    xf = x.astype(jnp.float32)
    y = xf * lax.rsqrt(jnp.mean(xf * xf, axis=-1, keepdims=True) + eps)
    return (y * w.astype(jnp.float32)).astype(x.dtype)

def l2norm(x, eps=1e-6):
    xf = x.astype(jnp.float32)
    return xf * lax.rsqrt(jnp.sum(xf * xf, axis=-1, keepdims=True) + eps)

def token_shift(x):
    return jnp.pad(x, ((0, 0), (1, 0), (0, 0)))[:, :-1]

def causal_depthwise_conv(x, w):
    k_width, chans = w.shape
    return lax.conv_general_dilated(
        x, w[:, None, :].astype(x.dtype), window_strides=(1,),
        padding=[(k_width - 1, 0)], dimension_numbers=('NWC', 'WIO', 'NWC'),
        feature_group_count=chans)

def rwkv7_recurrence(r, w, k, v, a, b):
    bsz, _, heads, n = r.shape

    def step(state, inp):
        r_t, w_t, k_t, v_t, a_t, b_t = inp
        sa = jnp.einsum('bhvk,bhk->bhv', state, a_t)
        state = (state * w_t[:, :, None, :] + sa[..., None] * b_t[:, :, None, :]
                 + v_t[..., None] * k_t[:, :, None, :])
        return state, jnp.einsum('bhvk,bhk->bhv', state, r_t)

    xs = tuple(jnp.moveaxis(t, 1, 0) for t in (r, w, k, v, a, b))
    s0 = jnp.zeros((bsz, heads, n, n), jnp.float32)
    _, y = lax.scan(step, s0, xs)
    return jnp.moveaxis(y, 0, 1)

def gated_delta_rule_chunked(q, k, v, g, beta):
    bsz, seq, heads, dk = q.shape
    dv = v.shape[-1]
    n_chunks = seq // CHUNK

    def blocks(t):
        t = t.reshape((bsz, n_chunks, CHUNK, heads) + t.shape[3:])
        return jnp.moveaxis(t, 3, 1)

    q, k, v, g, beta = blocks(q), blocks(k), blocks(v), blocks(g), blocks(beta)
    gc = jnp.cumsum(g, axis=-1)
    causal = jnp.tril(jnp.ones((CHUNK, CHUNK), bool))
    strict = jnp.tril(jnp.ones((CHUNK, CHUNK), bool), -1)
    decay = jnp.exp(jnp.where(causal, gc[..., :, None] - gc[..., None, :], -jnp.inf))
    kb = k * beta[..., None]
    vb = v * beta[..., None]
    lower = jnp.where(strict, jnp.einsum('bhncd,bhnsd->bhncs', kb, k) * decay, 0.0)
    eye = jnp.eye(CHUNK, dtype=q.dtype)
    tmat = lax.linalg.triangular_solve(eye + lower, jnp.broadcast_to(eye, lower.shape),
                                       left_side=True, lower=True)
    u = tmat @ vb
    wk = tmat @ (kb * jnp.exp(gc)[..., None])
    qk = jnp.einsum('bhncd,bhnsd->bhncs', q, k) * decay
    q_dec = q * jnp.exp(gc)[..., None]
    k_dec = k * jnp.exp(gc[..., -1:] - gc)[..., None]
    g_last = jnp.exp(gc[..., -1])

    def step(state, inp):
        u_i, w_i, qk_i, qd_i, kd_i, gl_i = inp
        v_new = u_i - w_i @ state
        o_i = qd_i @ state + qk_i @ v_new
        state = state * gl_i[..., None, None] + jnp.swapaxes(kd_i, -1, -2) @ v_new
        return state, o_i

    xs = tuple(jnp.moveaxis(t, 2, 0) for t in (u, wk, qk, q_dec, k_dec, g_last))
    s0 = jnp.zeros((bsz, heads, dk, dv), jnp.float32)
    _, o = lax.scan(step, s0, xs)
    o = jnp.moveaxis(o, 0, 2)
    return jnp.moveaxis(o, 1, 3).reshape(bsz, seq, heads, dv)

def hybrid_layer(x, norm_mix_pre, norm_mix_post, norm_ffn_pre, norm_ffn_post, w_in,
                 rwkv_mix, rwkv_w0, rwkv_w2, rwkv_a0, rwkv_a2, rwkv_g2, rwkv_k_k, rwkv_k_a,
                 rwkv_r_k, rwkv_ln_w, rwkv_ln_b, gdn_conv_w, gdn_a_log, gdn_dt_bias,
                 gdn_norm_w, w_out, ffn_w_gate, ffn_w_up, ffn_w_down):
    bsz, seq, d = x.shape
    f32 = jnp.float32
    rwkv_heads = lambda t: t.reshape(bsz, seq, RWKV_HEADS, RWKV_HEAD_DIM)
    gdn_heads = lambda t: t.reshape(bsz, seq, GDN_HEADS, GDN_HEAD_DIM)

    xn = rmsnorm(x, norm_mix_pre)
    p = (xn @ w_in).astype(f32)
    p_rwkv, p_qkv, p_z, p_beta, p_alpha, p_gate_a, p_gate_b = _split(p, IN_SPLITS)

    p_rwkv = p_rwkv + (token_shift(p_rwkv) - p_rwkv) * rwkv_mix.astype(f32)
    r, k, v, lw, la, lg = _split(p_rwkv, RWKV_SPLITS)
    w_log = -jax.nn.softplus(-(rwkv_w0.astype(f32) + jnp.tanh(lw) @ rwkv_w2.astype(f32))) - 0.5
    decay = jnp.exp(-jnp.exp(w_log))
    a = jax.nn.sigmoid(rwkv_a0.astype(f32) + la @ rwkv_a2.astype(f32))
    out_gate = jax.nn.sigmoid(lg) @ rwkv_g2.astype(f32)
    kk = l2norm(rwkv_heads(k * rwkv_k_k.astype(f32)))
    k = k * (1.0 + (a - 1.0) * rwkv_k_a.astype(f32))
    rh, kh, vh, ah = rwkv_heads(r), rwkv_heads(k), rwkv_heads(v), rwkv_heads(a)
    y = rwkv7_recurrence(rh, rwkv_heads(decay), kh, vh, -kk, kk * ah)
    mu = jnp.mean(y, axis=-1, keepdims=True)
    var = jnp.mean(jnp.square(y - mu), axis=-1, keepdims=True)
    y = ((y - mu) * lax.rsqrt(var + RWKV_GN_EPS)).reshape(bsz, seq, d) * rwkv_ln_w.astype(f32) + rwkv_ln_b.astype(f32)
    bonus = jnp.sum(rh * kh * rwkv_r_k.astype(f32), axis=-1, keepdims=True) * vh
    y_a = (y + bonus.reshape(bsz, seq, d)) * out_gate

    qkv = jax.nn.silu(causal_depthwise_conv(p_qkv, gdn_conv_w.astype(f32)))
    q, k, v = _split(qkv, (d, d, d))
    q = l2norm(gdn_heads(q)) * GDN_HEAD_DIM ** -0.5
    k = l2norm(gdn_heads(k))
    beta = jax.nn.sigmoid(p_beta)
    g = -jnp.exp(gdn_a_log.astype(f32)) * jax.nn.softplus(p_alpha + gdn_dt_bias.astype(f32))
    o = gated_delta_rule_chunked(q, k, gdn_heads(v), g, beta)
    o = rmsnorm(o, gdn_norm_w) * jax.nn.silu(gdn_heads(p_z))
    y_b = o.reshape(bsz, seq, d)

    mixed = jax.nn.sigmoid(p_gate_a) * y_a + jax.nn.sigmoid(p_gate_b) * y_b
    x = x + rmsnorm(mixed.astype(x.dtype) @ w_out, norm_mix_post)

    xn = rmsnorm(x, norm_ffn_pre)
    hidden = jax.nn.silu(xn @ ffn_w_gate) * (xn @ ffn_w_up)
    return x + rmsnorm(hidden @ ffn_w_down, norm_ffn_post)

def setup_inputs(seed: int = 0) -> dict:
    key = jax.random.key(seed)
    ks = jax.random.split(key, 26)
    L, D = DEPTH, D_MODEL
    nrm = lambda kk, shape, s: s * jax.random.normal(kk, shape, jnp.float32)
    gain = lambda kk, shape: 1.0 + nrm(kk, shape, 0.05)
    dt = jnp.exp(jax.random.uniform(ks[21], (L, GDN_HEADS), jnp.float32, math.log(1e-3), math.log(1e-1)))
    return {
        'x': nrm(ks[0], (BATCH, SEQ, D), 1.0),
        'norm_mix_pre': gain(ks[1], (L, D)),
        'norm_mix_post': gain(ks[2], (L, D)),
        'norm_ffn_pre': gain(ks[3], (L, D)),
        'norm_ffn_post': gain(ks[4], (L, D)),
        'w_in': nrm(ks[5], (L, D, IN_COLS), D ** -0.5),
        'rwkv_mix': jax.random.uniform(ks[6], (L, RWKV_COLS), jnp.float32),
        'rwkv_w0': jnp.linspace(-5.0, 1.0, D, dtype=jnp.float32)[None, :] + nrm(ks[7], (L, D), 0.1),
        'rwkv_w2': nrm(ks[8], (L, RWKV_DECAY_LORA, D), 0.1 * RWKV_DECAY_LORA ** -0.5),
        'rwkv_a0': nrm(ks[9], (L, D), 0.1),
        'rwkv_a2': nrm(ks[10], (L, RWKV_AAA_LORA, D), 0.1 * RWKV_AAA_LORA ** -0.5),
        'rwkv_g2': nrm(ks[11], (L, RWKV_GATE_LORA, D), RWKV_GATE_LORA ** -0.5),
        'rwkv_k_k': 0.85 + nrm(ks[12], (L, D), 0.05),
        'rwkv_k_a': gain(ks[13], (L, D)),
        'rwkv_r_k': nrm(ks[14], (L, RWKV_HEADS, RWKV_HEAD_DIM), 0.1),
        'rwkv_ln_w': gain(ks[15], (L, D)),
        'rwkv_ln_b': nrm(ks[16], (L, D), 0.02),
        'gdn_conv_w': nrm(ks[17], (L, GDN_CONV, 3 * D), GDN_CONV ** -0.5),
        'gdn_a_log': jnp.log(jax.random.uniform(ks[18], (L, GDN_HEADS), jnp.float32, 1.0, 16.0)),
        'gdn_dt_bias': dt + jnp.log(-jnp.expm1(-dt)),
        'gdn_norm_w': gain(ks[19], (L, GDN_HEAD_DIM)),
        'w_out': nrm(ks[20], (L, D, D), D ** -0.5),
        'ffn_w_gate': nrm(ks[22], (L, D, D_FF), D ** -0.5),
        'ffn_w_up': nrm(ks[23], (L, D, D_FF), D ** -0.5),
        'ffn_w_down': nrm(ks[24], (L, D_FF, D), D_FF ** -0.5),
    }

def reference(x, norm_mix_pre, norm_mix_post, norm_ffn_pre, norm_ffn_post, w_in,
              rwkv_mix, rwkv_w0, rwkv_w2, rwkv_a0, rwkv_a2, rwkv_g2, rwkv_k_k, rwkv_k_a,
              rwkv_r_k, rwkv_ln_w, rwkv_ln_b, gdn_conv_w, gdn_a_log, gdn_dt_bias,
              gdn_norm_w, w_out, ffn_w_gate, ffn_w_up, ffn_w_down):
    h = x
    for l in range(DEPTH):
        h = hybrid_layer(h, norm_mix_pre[l], norm_mix_post[l], norm_ffn_pre[l], norm_ffn_post[l],
                         w_in[l], rwkv_mix[l], rwkv_w0[l], rwkv_w2[l], rwkv_a0[l], rwkv_a2[l],
                         rwkv_g2[l], rwkv_k_k[l], rwkv_k_a[l], rwkv_r_k[l], rwkv_ln_w[l],
                         rwkv_ln_b[l], gdn_conv_w[l], gdn_a_log[l], gdn_dt_bias[l],
                         gdn_norm_w[l], w_out[l], ffn_w_gate[l], ffn_w_up[l], ffn_w_down[l])
    return h


_drawn_inputs = setup_inputs


def setup_inputs(seed=0):
    import zlib

    import numpy as np

    out = dict(_drawn_inputs(seed))
    spreads = {}
    factors = {'rwkv_w2': 8.0, 'rwkv_k_k': 4.411, 'rwkv_ln_b': 5.102}
    for name, (base, spread) in spreads.items():
        noise = np.random.default_rng([zlib.crc32(name.encode()), seed]).standard_normal(out[name].shape)
        drawn = base * np.exp(spread * noise) if base else spread * noise
        out[name] = jnp.asarray(drawn.astype(out[name].dtype))
    for name, factor in factors.items():
        out[name] = (out[name] * factor).astype(out[name].dtype)
    return out
```

```python
from contextlib import ExitStack
import math

import numpy as np
import concourse.bass as bass
from concourse import mybir

F32 = mybir.dt.float32
F32R = mybir.dt.float32r
I32 = mybir.dt.int32
ALU = mybir.AluOpType
ACT = mybir.ActivationFunctionType
AX = mybir.AxisListType

P = 128
D = 2048
T = 256
NT = T // P
KC = D // P
NU = D // P
CH = 64
RH = 64
FF = 5632
FB = FF // 512
FKC = FF // P
LORA_W, LORA_A, LORA_G = 96, 96, 256
COL_LORA = 3 * D
COL_QKV = 3 * D + LORA_W + LORA_A + LORA_G
COL_Z = COL_QKV + 3 * D
COL_BETA = COL_Z + D
COL_GATE = COL_BETA + 32
NORM_EPS = 1e-6
GN_EPS = 64e-5
KAPPA = math.exp(-0.5)

PW = 384
QU = 24
QL = 16

(MIX_R, MIX_K, MIX_V, W0, A0, K_K, K_A, R_K) = range(8)
TAP = (8, 11, 16, 19)
NORM1, NORM2 = 14, 15
OMM, OKA, HW0, HA0 = 22, 25, 26, 27
NPAR = 28


class Steps:

    def __init__(self, sem, names):
        self.sem, self.names, self.n, self.next = sem, list(names), len(names), 0
        assert len(set(names)) == len(names)

    def at(self, name):
        assert self.names[self.next] == name, (name, self.names[self.next])
        self.next = (self.next + 1) % self.n
        return 1

    def after(self, name, unit=0):
        return unit * self.n + self.names.index(name) + 1


    def step(self, name, ins):
        ins.then_inc(self.sem, self.at(name))


def rsqrt_names(tag):
    return [f"{tag}{i}" for i in range(11)]


def rsqrt(nc, dve, done, tag, unit, y, v, t):
    names = iter(rsqrt_names(tag))

    def step(ins):
        name = next(names)
        done.step(name, ins)
        dve.wait_ge(done.sem, done.after(name, unit))

    step(nc.vector.tensor_scalar(y.bitcast(I32), v.bitcast(I32), -0.5, 1597463007.0, ALU.mult, ALU.add))
    step(nc.vector.tensor_scalar(v, v, -0.5, None, ALU.mult))
    for _ in range(3):
        step(nc.vector.tensor_tensor(t, y, y, ALU.mult))
        step(nc.vector.tensor_tensor(t, t, v, ALU.mult))
        step(nc.vector.scalar_tensor_tensor(y, t, 1.5, y, ALU.add, ALU.mult))


def build(nc, a, out):
    with ExitStack() as ctx:
        def sb(name, shape, dt=F32, c=ctx):
            return c.enter_context(nc.sbuf_tensor(name, shape, dt))

        def sem(name):
            return ctx.enter_context(nc.semaphore(name))

        ps = ctx.enter_context(nc.psum_tensor("ps", [P, 8, 512], F32))
        xh = sb("xh", [P, KC, T], F32R)
        xl = sb("xl", [P, KC, T], F32R)
        ident = sb("ident", [P, P])
        par = sb("par", [P, NPAR, NU])
        par2 = par[:].rearrange("p a b -> p (a b)")
        keep = sb("keep", [P, KC, T])
        mixT = keep

        weights_in = [sem(f"weights_in{i}") for i in range(3)]
        small_in = sem("small_in")
        x_in = sem("x_in")
        masks_made = sem("masks_made")
        hi_ready, lo_ready = sem("hi_ready"), sem("lo_ready")
        quantum_done, pass_out = sem("quantum_done"), sem("pass_out")
        pe_sem, act_sem, dve_sem, pool_sem = sem("pe_mix"), sem("act_mix"), sem("dve_mix"), sem("pool_mix")
        lora_in, gate_in, ln_in = sem("lora_in"), sem("gate_in"), sem("ln_in")

        w_in3 = a["w_in"][0].rearrange("(kc p) n -> p kc n", p=P)

        mix_ctx = ctx.enter_context(ExitStack())

        def mb(name, shape, dt=F32):
            return sb(name, shape, dt, mix_ctx)

        raw = [mb(f"raw{i}", [P, 8, PW]) for i in range(3)]
        hi = [mb(f"hi{i}", [P, 2, PW], F32R) for i in range(2)]
        lo = [mb(f"lo{i}", [P, 2, PW], F32R) for i in range(2)]
        tlw = mb("tlw", [LORA_W, T])
        tla = mb("tla", [LORA_A, T])
        tlg = mb("tlg", [P, 2, T])
        bg = mb("bg", [P, NT, 2, NU])
        cum_up = mb("cum_up", [P, P])
        strict_up = mb("strict_up", [P, P])
        strict_lo = mb("strict_lo", [P, P])
        m4 = mb("m4", [P, 4, P])
        lev = mb("lev", [P, 7, P])
        ones = mb("ones", [P, 1])
        halves = mb("halves", [P, 1])
        headsel = mb("headsel", [P, 2])
        eps4 = mb("eps4", [P, 4])
        st_scale = mb("st_scale", [P, 6])
        st_eps = mb("st_eps", [P, 6])
        restart = mb("restart", [P, T])
        gnw = mb("gnw", [P, P])

        def columns(j, u):
            if j == 0:
                return [u * P, D + u * P, 2 * D + u * P]
            if j == 1:
                return [COL_QKV + u * P, COL_QKV + D + u * P, COL_QKV + 2 * D + u * P]
            return [COL_Z + u * P, COL_GATE + u * P, COL_GATE + D + u * P]

        def load_unit_weights(sp, u):
            for i in range(6):
                j, half = i // 2, i % 2
                fill = 4 + i
                sp.wait_ge(lo_ready, 24 * u + 4 * fill - 8)
                for seg, col in enumerate(columns(j, u)):
                    sp.dma_start(raw[fill % 3][:, :, seg * P:(seg + 1) * P],
                                 w_in3[:, 8 * half:8 * half + 8, bass.ds(col, P)]
                                 ).then_inc(weights_in[fill % 3], 16)

        def split_hi(act, u, q, w=PW):
            base = 0 if u is None else QL + QU * u
            fill = q // 4 + (0 if u is None else 4)
            arrived = 48 * (fill // 3 + 1) + (0 if u is None else 96 * u)
            act.wait_ge(weights_in[fill % 3], arrived)
            if not (u is None and q < 2):
                act.wait_ge(quantum_done, base + q - 1)
            nc.scalar.activation(hi[q % 2][:, :, 0:w], raw[fill % 3][:, 2 * (q % 4):2 * (q % 4) + 2, 0:w],
                                 ACT.Copy).then_inc(hi_ready, 1)

        def split_lo(dve, u, q, w=PW):
            base = 0 if u is None else QL + QU * u
            fill = q // 4 + (0 if u is None else 4)
            dve.wait_ge(hi_ready, base + q + 1)
            nc.vector.tensor_tensor(lo[q % 2][:, :, 0:w], raw[fill % 3][:, 2 * (q % 4):2 * (q % 4) + 2, 0:w],
                                    hi[q % 2][:, :, 0:w].bitcast(F32), ALU.subtract).then_inc(lo_ready, 1)

        def project(pe, u, q, w=PW):
            base = 0 if u is None else QL + QU * u
            j = q // 8
            if q % 8 == 0:
                if u is not None:
                    pe.wait_ge(pass_out, 3 * u + 2 + (0 if j == 0 else j - 1))
            pe.wait_ge(lo_ready, base + q + 1)
            for k in range(2):
                kc = 2 * (q % 8) + k
                for t in range(NT):
                    o = ps[:, 4 + 2 * (j % 2) + t, 0:w]
                    xs = slice(t * P, (t + 1) * P)
                    nc.tensor.matmul(o, xh[:, kc, xs], hi[q % 2][:, k, 0:w], start=kc == 0, stop=False)
                    nc.tensor.matmul(o, xh[:, kc, xs], lo[q % 2][:, k, 0:w], start=False, stop=False)
                    last = nc.tensor.matmul(o, xl[:, kc, xs], hi[q % 2][:, k, 0:w],
                                            start=False, stop=kc == KC - 1)
            last.then_inc(quantum_done, 1)

        def pass_columns(u, j):
            return 2 + 3 * u + j + 1

        G8 = range(KC // 2)
        pre_dve = Steps(sem("pre_dve"), ["var"] + rsqrt_names("rs") + ["par"] + [f"lo{g}" for g in G8]
                        + ["omm", "oka", "hw0", "ha0", "lomm0", "lomm1", "lomm2", "lomm3", "gnw"]
                        + ["shift0", "shift1", "shift2", "shift3", "tlg", "beta", "y", "ymax", "yabs", "sp", "g"])
        pre_act = Steps(sem("pre_act"), ["ss0", "ss1", "xs0", "xs1"] + [f"hi{g}" for g in G8]
                        + ["un0", "un1", "un2", "un3", "tlw", "tla", "tlg", "beta", "alog", "exp", "ln"])
        pre_pe = Steps(sem("pre_pe"), ["par"] + [f"x{g}" for g in G8] + ["lora"])

        def transpose_x_pe(pe, done, src, read_out):
            for g in G8:
                if g >= 4:
                    pe.wait_ge(read_out.sem, read_out.after(f"lo{g - 4}"))
                for k in range(2):
                    for t in range(NT):
                        last = nc.tensor.transpose(ps[:, g % 4, k * T + t * P:k * T + (t + 1) * P],
                                                   src[:, t, (2 * g + k) * P:(2 * g + k + 1) * P], ident[:])
                done.step(f"x{g}", last)

        def transpose_x_act(act, done, turned, weight):
            for g in G8:
                act.wait_ge(turned.sem, turned.after(f"x{g}"))
                for k in range(2):
                    kc = 2 * g + k
                    last = nc.scalar.activation(xh[:, kc, :], ps[:, g % 4, k * T:(k + 1) * T], ACT.Copy,
                                                scale=par[:, weight, kc:kc + 1])
                done.step(f"hi{g}", last)

        def transpose_x_dve(dve, done, high, weight):
            for g in G8:
                dve.wait_ge(high.sem, high.after(f"hi{g}"))
                for k in range(2):
                    kc = 2 * g + k
                    last = nc.vector.scalar_tensor_tensor(
                        xl[:, kc, :], ps[:, g % 4, k * T:(k + 1) * T], par[:, weight, kc:kc + 1],
                        xh[:, kc, :].bitcast(F32), ALU.mult, ALU.subtract)
                done.step(f"lo{g}", last)

        w2s = mb("w2s", [LORA_W, P])
        a2s = mb("a2s", [LORA_A, P])
        g2s = mb("g2s", [P, 2, P])
        lnw = mb("lnw", [P, P])
        lnb = mb("lnb", [P, P])

        def load_lora(eng, u):
            eng.dma_start(w2s[:], a["rwkv_w2"][0][:, bass.ds(u * P, P)]).then_inc(lora_in, 16)
            eng.dma_start(a2s[:], a["rwkv_a2"][0][:, bass.ds(u * P, P)]).then_inc(lora_in, 16)

        def load_gate(eng, u):
            g2 = a["rwkv_g2"][0].rearrange("(k p) n -> p k n", p=P)
            eng.dma_start(g2s[:], g2[:, :, bass.ds(u * P, P)]).then_inc(gate_in, 16)

        def load_ln(eng, u):
            for dst, src in ((lnw, "rwkv_ln_w"), (lnb, "rwkv_ln_b")):
                eng.dma_start(dst[:], a[src][0][bass.ds(u * P, P)].partition_broadcast(P)).then_inc(ln_in, 16)

        N_SMALL = 21
        with ExitStack() as c1:
            def tb(name, shape, dt=F32):
                return sb(name, shape, dt, c1)

            xt = tb("xt", [P, NT, D])
            junk = tb("junk", [P, D])
            prow = [tb(f"prow{i}", [P, P]) for i in range(3)]
            ss = tb("ss", [P, NT])
            rx = tb("rx", [P, NT])
            rt = tb("rt", [P, NT])
            lp = tb("lp", [P, NT, 480])
            lmix = tb("lmix", [P, 4])
            lomm = tb("lomm", [P, 4])
            lf = tb("lf", [P, 4, T])
            alog = tb("alog", [P, NU])
            dtb = tb("dtb", [P, NU])
            sp1 = tb("sp1", [P, NT, NU])
            sp2 = tb("sp2", [P, NT, NU])
            lora_cols = ((0, LORA_W), (LORA_W, LORA_A), (LORA_W + LORA_A, P), (LORA_W + LORA_A + P, P))

            with nc.Block() as block:
                @block.sync
                def _(sp):
                    sp.dma_start(xt[:], a["x"][0].rearrange("(t p) n -> p t n", p=P)).then_inc(x_in, 16)

                    def rows(v):
                        return v.rearrange("(u p) -> u p", p=P)

                    mix = a["rwkv_mix"][0]
                    vecs = [mix[0:D], mix[D:2 * D], mix[2 * D:3 * D], a["rwkv_w0"][0], a["rwkv_a0"][0],
                            a["rwkv_k_k"][0], a["rwkv_k_a"][0], a["rwkv_r_k"][0].rearrange("h n -> (h n)")]
                    for i, v in enumerate(vecs):
                        sp.dma_start(prow[0][16 * i:16 * i + 16, :], rows(v)).then_inc(small_in, 16)
                    conv = a["gdn_conv_w"][0]
                    for i in range(2):
                        sp.dma_start(prow[1][48 * i:48 * i + 48, :], rows(conv[i])).then_inc(small_in, 16)
                        sp.dma_start(prow[2][48 * i:48 * i + 48, :], rows(conv[2 + i])).then_inc(small_in, 16)
                    sp.dma_start(prow[1][96:112, :], rows(a["norm_mix_pre"][0])).then_inc(small_in, 16)
                    sp.dma_start(prow[1][112:128, :], rows(a["norm_ffn_pre"][0])).then_inc(small_in, 16)
                    with nc.allow_non_contiguous_dma(reason="a few hundred single values"):
                        for i, (c0, n) in enumerate(lora_cols):
                            sp.dma_start(lmix[0:n, i:i + 1],
                                         mix[3 * D + c0:3 * D + c0 + n].rearrange("(p a) -> p a", a=1)
                                         ).then_inc(small_in, 16)
                    sp.dma_start(alog[:], a["gdn_a_log"][0].partition_broadcast(P)).then_inc(small_in, 16)
                    sp.dma_start(dtb[:], a["gdn_dt_bias"][0].partition_broadcast(P)).then_inc(small_in, 16)
                    sp.dma_start(gnw[:], a["gdn_norm_w"][0].partition_broadcast(P)).then_inc(small_in, 16)
                    load_lora(sp, 0)
                    load_gate(sp, 0)
                    load_ln(sp, 0)
                    for fill in range(4):
                        j, half = fill // 2, fill % 2
                        if fill >= 3:
                            sp.wait_ge(lo_ready, 4 * fill - 8)
                        segs = ([(0, COL_LORA, P), (P, COL_LORA + P, P), (2 * P, COL_LORA + 2 * P, P)] if j == 0
                                else [(0, COL_LORA + PW, 64), (64, COL_BETA, 16), (80, COL_BETA + 16, 16)])
                        for at, col, n in segs:
                            sp.dma_start(raw[fill % 3][:, :, at:at + n],
                                         w_in3[:, 8 * half:8 * half + 8, col:col + n]
                                         ).then_inc(weights_in[fill % 3], 16)

                @block.gpsimd
                def _(pool):
                    made = [0]

                    def chain(ins):
                        made[0] += 1
                        ins.then_inc(masks_made, 1)
                        pool.wait_ge(masks_made, made[0])

                    def keep(tile, pattern, base, cm, op=ALU.is_ge, fill=0.0):
                        chain(nc.gpsimd.affine_select(out=tile, in_=tile, compare_op=op, fill=fill, base=base,
                                                      pattern=pattern, channel_multiplier=cm))

                    def chunks(tile):
                        return tile.rearrange("p (b j) -> p b j", j=CH)

                    chain(nc.gpsimd.memset(ident[:], 0.0))
                    keep(ident[:], [[-1, P]], 0, 1, ALU.not_equal, 1.0)
                    for tile, base in ((cum_up, 0), (strict_up, -1)):
                        chain(nc.gpsimd.memset(tile[:], 1.0))
                        keep(chunks(tile[:]), [[CH, 2], [1, CH]], base, -1)
                        keep(chunks(tile[:]), [[-CH, 2], [0, CH]], 0, 1)
                    chain(nc.gpsimd.memset(strict_lo[:], 1.0))
                    keep(chunks(strict_lo[:]), [[-CH, 2], [-1, CH]], -1, 1)
                    keep(chunks(strict_lo[:]), [[CH, 2], [0, CH]], CH - 1, -1)
                    for i in range(6):
                        m = 1 << i
                        nb = P // (2 * m)
                        v = lev[:, i, :].rearrange("p (b e j) -> p b e j", e=2, j=m)
                        chain(nc.gpsimd.memset(lev[:, i, :], 0.0))
                        chain(nc.gpsimd.memset(v[:, :, 0, :], 1.0))
                        keep(v[:, :, 0, :], [[-2 * m, nb], [0, m]], -m, 1)
                        keep(v[:, :, 0, :], [[2 * m, nb], [0, m]], 2 * m - 1, -1)
                    v = lev[:, 6, :].rearrange("p (b e) -> p b e", e=2)
                    chain(nc.gpsimd.memset(lev[:, 6, :], 0.0))
                    keep(v[:, :, 1], [[-2, P // 2]], 0, 1, ALU.not_equal, 1.0)
                    chain(nc.gpsimd.memset(ones[:], 1.0))
                    chain(nc.gpsimd.memset(halves[:], 0.5))
                    chain(nc.gpsimd.memset(headsel[:], 1.0))
                    keep(headsel[:, 0:1], [[0, 1]], RH - 1, -1)
                    keep(headsel[:, 1:2], [[0, 1]], -RH, 1)
                    chain(nc.gpsimd.memset(restart[:], 1.0))
                    chain(nc.gpsimd.memset(restart[:].rearrange("p (c j) -> p c j", j=CH)[:, :, 0:1], 0.0))
                    nc.gpsimd.memset(eps4[:, 0:2], 1e-6)
                    nc.gpsimd.memset(eps4[:, 2:4], 4e-6)
                    nc.gpsimd.memset(st_scale[:, 0:4], 1.0 / RH)
                    nc.gpsimd.memset(st_scale[:, 4:6], 1.0 / P)
                    nc.gpsimd.memset(st_eps[:, 0:4], GN_EPS)
                    nc.gpsimd.memset(st_eps[:, 4:6], NORM_EPS)
                    for i, msk in enumerate((strict_up, cum_up, strict_up, cum_up)):
                        nc.gpsimd.tensor_copy(m4[:, i, :], msk[:])

                @block.scalar
                def _(act):
                    A, D_, Pe = pre_act, pre_dve, pre_pe
                    act.wait_ge(x_in, 16)
                    for t in range(NT):
                        if t:
                            act.wait_ge(A.sem, A.after("ss0"))
                        A.step(f"ss{t}", nc.scalar.activation(junk[:], xt[:, t, :], ACT.Square,
                                                              accum_out=ss[:, t:t + 1]))
                    act.wait_ge(D_.sem, D_.after("rs10"))
                    for t in range(NT):
                        A.step(f"xs{t}", nc.scalar.activation(xt[:, t, :], xt[:, t, :], ACT.Copy,
                                                              scale=rx[:, t:t + 1]))
                    act.wait_ge(D_.sem, D_.after("par"))
                    transpose_x_act(act, A, Pe, NORM1)
                    for q in range(QL):
                        split_hi(act, None, q, PW if q < 8 else 96)
                    for j, w in ((0, PW), (1, 96)):
                        act.wait_ge(quantum_done, 8 * (j + 1))
                        for t in range(NT):
                            last = nc.scalar.activation(lp[:, t, PW * j:PW * j + w], ps[:, 4 + 2 * j + t, 0:w],
                                                        ACT.Copy)
                        last.then_inc(pass_out, 1)
                    act.wait_ge(Pe.sem, Pe.after("lora"))
                    act.wait_ge(D_.sem, D_.after("lomm3"))
                    for i, (_, n) in enumerate(lora_cols):
                        A.step(f"un{i}", nc.scalar.activation(
                            lf[0:n, i, :], ps[0:n, i // 2, (i % 2) * T:(i % 2 + 1) * T], ACT.Copy,
                            scale=lomm[0:n, i:i + 1]))
                    act.wait_ge(D_.sem, D_.after("shift3"))
                    A.step("tlw", nc.scalar.activation(tlw[:], lf[0:LORA_W, 0, :], ACT.Tanh))
                    A.step("tla", nc.scalar.activation(tla[:], lf[0:LORA_A, 1, :], ACT.Copy))
                    A.step("tlg", nc.scalar.activation(tlg[:], lf[:, 2:4, :], ACT.Tanh, scale=0.5))
                    act.wait_ge(pass_out, 2)
                    A.step("beta", nc.scalar.activation(bg[:, :, 0, :], lp[:, :, 448:464], ACT.Tanh, scale=0.5))
                    A.step("alog", nc.scalar.activation(alog[:], alog[:], ACT.Exp))
                    act.wait_ge(D_.sem, D_.after("yabs"))
                    A.step("exp", nc.scalar.activation(sp1[:], sp1[:], ACT.Exp))
                    act.wait_ge(A.sem, A.after("exp"))
                    A.step("ln", nc.scalar.activation(sp1[:], sp1[:], ACT.Ln, bias=1.0))

                @block.vector
                def _(dve):
                    A, D_, Pe = pre_act, pre_dve, pre_pe

                    def step(name, ins):
                        D_.step(name, ins)
                        dve.wait_ge(D_.sem, D_.after(name))

                    dve.wait_ge(A.sem, A.after("ss1"))
                    step("var", nc.vector.tensor_scalar(ss[:], ss[:], 1.0 / D, NORM_EPS, ALU.mult, ALU.add))
                    rsqrt(nc, dve, D_, "rs", 0, rx[:], ss[:], rt[:])
                    dve.wait_ge(Pe.sem, Pe.after("par"))
                    step("par", nc.vector.tensor_copy(par2[:, 0:352], ps[:, 0, 0:352]))
                    transpose_x_dve(dve, D_, A, NORM1)
                    for name, src, dst, num, f0, f1 in (("omm", MIX_R, OMM, 3, -1.0, 1.0), ("oka", K_A, OKA, 1, -1.0, 1.0),
                                                        ("hw0", W0, HW0, 1, 0.5, 0.0), ("ha0", A0, HA0, 1, 0.5, 0.0)):
                        step(name, nc.vector.tensor_scalar(par[:, dst:dst + num, :], par[:, src:src + num, :], f0, f1,
                                                           ALU.mult, ALU.add))
                    dve.wait_ge(small_in, 16 * N_SMALL)
                    for i, (_, n) in enumerate(lora_cols):
                        step(f"lomm{i}", nc.vector.tensor_scalar(lomm[0:n, i:i + 1], lmix[0:n, i:i + 1], -1.0, 1.0,
                                                                 ALU.mult, ALU.add))
                    step("gnw", nc.vector.tensor_scalar(gnw[:], gnw[:], 0.25, None, ALU.mult))
                    for q in range(QL):
                        split_lo(dve, None, q, PW if q < 8 else 96)
                    dve.wait_ge(A.sem, A.after("un3"))
                    for i, (_, n) in enumerate(lora_cols):
                        src = ps[0:n, i // 2, (i % 2) * T:(i % 2 + 1) * T]
                        step(f"shift{i}", nc.vector.scalar_tensor_tensor(
                            lf[0:n, i, 1:T], src[:, 0:T - 1], lmix[0:n, i:i + 1], lf[0:n, i, 1:T],
                            ALU.mult, ALU.add))
                    dve.wait_ge(A.sem, A.after("beta"))
                    step("tlg", nc.vector.tensor_scalar(tlg[:], tlg[:], 0.5, 0.5, ALU.mult, ALU.add))
                    step("beta", nc.vector.tensor_scalar(bg[:, :, 0, :], bg[:, :, 0, :], 0.5, 0.5, ALU.mult, ALU.add))
                    step("y", nc.vector.tensor_tensor(sp2[:], lp[:, :, 464:480],
                                                      dtb[:].unsqueeze(1).to_broadcast([P, NT, NU]), ALU.add))
                    step("ymax", nc.vector.tensor_scalar(sp1[:], sp2[:], 0.0, -2.0, ALU.max, ALU.mult))
                    step("yabs", nc.vector.tensor_tensor(sp1[:], sp1[:], sp2[:], ALU.add))
                    dve.wait_ge(A.sem, A.after("ln"))
                    step("sp", nc.vector.scalar_tensor_tensor(sp2[:], sp2[:], 0.0, sp1[:], ALU.max, ALU.add))
                    step("g", nc.vector.scalar_tensor_tensor(
                        bg[:, :, 1, :], sp2[:], -1.0, alog[:].unsqueeze(1).to_broadcast([P, NT, NU]),
                        ALU.mult, ALU.mult))

                @block.tensor
                def _(pe):
                    A, D_, Pe = pre_act, pre_dve, pre_pe
                    pe.wait_ge(masks_made, 2)
                    pe.wait_ge(small_in, 16 * N_SMALL)
                    for i, nr in enumerate((P, P, 96)):
                        last = nc.tensor.transpose(ps[:, 0, P * i:P * i + nr], prow[i][0:nr, :], ident[0:nr, 0:nr])
                    Pe.step("par", last)
                    pe.wait_ge(D_.sem, D_.after("par"))
                    pe.wait_ge(A.sem, A.after("xs1"))
                    transpose_x_pe(pe, Pe, xt, D_)
                    pe.wait_ge(D_.sem, D_.after("lo7"))
                    for q in range(QL):
                        project(pe, None, q, PW if q < 8 else 96)
                    pe.wait_ge(pass_out, 2)
                    for i, (c0, n) in enumerate(lora_cols):
                        for t in range(NT):
                            last = nc.tensor.transpose(
                                ps[0:n, i // 2, (i % 2) * T + t * P:(i % 2) * T + (t + 1) * P],
                                lp[:, t, c0:c0 + n], ident[:])
                    Pe.step("lora", last)

        with ExitStack() as c2:
            def tb(name, shape, dt=F32):
                return sb(name, shape, dt, c2)

            pu = tb("pu", [P, NT, 3 * PW])
            up = tb("up", [P, NPAR])
            ub = tb("ub", [P, NT, 2])
            uh = tb("uh", [P, NT])
            th = tb("th", [P, 3 * T])
            thg = th[:].rearrange("p (t c) -> p t c", t=NT)
            rkv = tb("rkv", [P, 3, T])
            qkv = tb("qkv", [P, 3, T])
            sq = tb("sq", [P, 3, T])
            sig = tb("sig", [P, T])
            cum = tb("cum", [P, T])
            wex = tb("wex", [P, T])
            winc = tb("winc", [P, T])
            winv = tb("winv", [P, T])
            al = tb("al", [P, T])
            kk = tb("kk", [P, T])
            kmod = tb("kmod", [P, T])
            prod = tb("prod", [P, T])
            ar = tb("ar", [P, 2, T])
            arh = tb("arh", [P, 2, 2, T])
            bhk = tb("bhk", [P, 2, T])
            kn = tb("kn", [P, T])
            kq = tb("kq", [P, 2, T])
            qde = tb("qde", [P, T])
            egr = tb("egr", [P, T])
            nrm = tb("nrm", [P, NT, 4])
            rn = tb("rn", [P, NT, 4])
            rtmp = tb("rtmp", [P, NT, 4])
            bon = tb("bon", [P, NT, 2])
            rne = tb("rne", [P, NT, P])
            gcc = tb("gcc", [P, NT])
            ege = tb("ege", [P, NT, 2])
            nege = tb("nege", [P, NT])
            dd = tb("dd", [P, NT, 2, P])
            dm = tb("dm", [P, NT, 3, P])
            vt = tb("vt", [P, NT, P])
            vp = [tb(f"vp{b}", [P, NT, P]) for b in range(2)]
            vb = tb("vb", [P, NT, P])
            bkt = tb("bkt", [P, 2, NT, P])
            kd = tb("kd", [P, NT, P])
            tr = tb("tr", [P, 4, 4, P])
            tg = tb("tg", [P, NT, 2, P])
            low = tb("low", [P, 6, P])
            xi = tb("xi", [P, 6, P])
            xt_ = tb("xit", [P, 6, P])
            yb = [tb(f"yb{i}", [P, 6, P]) for i in range(2)]
            rhs = tb("rhs", [P, 2, P])
            un = [tb(f"un{b}", [P, P]) for b in range(2)]
            vn = [tb(f"vn{b}", [P, P]) for b in range(2)]
            st = tb("st", [P, P])
            stw = tb("stw", [P, P])
            sg = tb("sg", [P, P])
            yy = tb("yy", [P, NT, P])
            oo = tb("oo", [P, NT, P])
            ga = tb("ga", [P, NT, P])
            gb = tb("gb", [P, NT, P])
            bv = tb("bv", [P, NT, P])
            ym = tb("ym", [P, 4])
            stt = tb("stt", [P, 6])
            rs = tb("rs", [P, 6])
            rst = tb("rst", [P, 6])

            LV = range(5)
            CN = range(T // CH)
            pe_names = (["tr1", "tr2", "lora", "norms", "rows", "tok", "in0", "in1", "in2", "in3", "nab", "g0", "g1"]
                        + [f"{x}{i}" for i in LV for x in "YX"]
                        + [f"c{k}_{c}" for c in CN for k in (1, 2, 3, 4) if not (k == 3 and c == 3)]
                        + ["gate", "mT"])
            act_names = (["gates", "ur", "uk", "uv", "cq", "ck", "cv", "tw", "ta", "sqk", "tq", "wex", "winv", "winc",
                          "sqq", "egr", "ege", "edt", "edl", "ah0", "ah1", "v", "vb0", "vb1", "bk", "kd0", "kd1"]
                         + [f"{x}{c}" for c in CN for x in ("r", "un", "y", "o")]
                         + ["ysq", "osq", "mT"])
            dve_names = (["ga", "gz", "gb", "sr", "sk", "sv"] + [f"c{j}{x}" for j in range(3) for x in "qkv"]
                         + ["kx", "sig", "al", "cum", "cex", "kf", "kmod", "rr0", "pr", "silu", "nrm", "bon"]
                         + rsqrt_names("n") + ["rq", "rkx", "gcc", "dt0", "dl0", "dt1", "dl1", "nege", "kk", "kn", "qn",
                                               "kb", "aw", "ap", "rr", "bh", "kh", "qde"]
                         + ["t0", "t1", "t2", "t3", "nab", "g0", "l0", "g1", "l1", "xm", "xi"]
                         + ["y0", "x0", "xt0", "y1", "x1", "xt1", "y2", "x2", "xt2", "y3", "x3", "xt3", "y4", "xt4"]
                         + ["vn0", "s0a", "s0b", "sg0", "g1c", "sw1", "vn1", "s1a", "s1b", "sg1",
                            "g2c", "sw2", "vn2", "s2a", "s2b", "sg2", "g3c", "vn3"]
                         + ["ys", "nm", "yc", "yv", "ov", "st1", "st2"] + rsqrt_names("r")
                         + ["yn", "ylw", "ybv", "yg", "yga", "mix"])
            pool_names = ["za", "zb", "up", "ub", "uh", "dm0", "dm1", "dml", "vp0", "vp1", "bv", "bvb",
                          "xtm", "xtg", "xti", "z0", "z1", "z2", "on", "onw", "ogb"]
            A, V, E, G = (Steps(act_sem, act_names), Steps(dve_sem, dve_names), Steps(pe_sem, pe_names),
                          Steps(pool_sem, pool_names))

            def cols(t):
                return slice(t * P, (t + 1) * P)

            def half(tile, m, odd):
                return tile.rearrange("p a (b e j) -> p a b e j", e=2, j=m)[:, :, :, odd, :]

            def half1(tile, m, odd):
                return tile.rearrange("p (b e j) -> p b e j", e=2, j=m)[:, :, odd, :]

            def mix_pe(pe, u, more):
                q_at = [0]

                def fill(n):
                    if more:
                        for _ in range(n):
                            project(pe, u + 1, q_at[0])
                            q_at[0] += 1

                def after(steps, name):
                    pe.wait_ge(steps.sem, steps.after(name, u))

                def mm(o, l, r, start=True, stop=True):
                    return nc.tensor.matmul(o, l, r, start=start, stop=stop, skip_group_check=True)

                pe.wait_ge(pass_out, pass_columns(u, 2))
                for i in range(3):
                    for t in range(NT):
                        last = nc.tensor.transpose(ps[:, i // 2, (i % 2) * T + t * P:(i % 2) * T + (t + 1) * P],
                                                   pu[:, t, i * P:(i + 1) * P], ident[:])
                E.step("tr1", last)
                for i in range(3):
                    for t in range(NT):
                        last = nc.tensor.transpose(ps[:, 2 + i // 2, (i % 2) * T + t * P:(i % 2) * T + (t + 1) * P],
                                                   pu[:, t, PW + i * P:PW + (i + 1) * P], ident[:])
                E.step("tr2", last)
                fill(3)
                pe.wait_ge(lora_in, 32 * u + 32)
                after(V, "sk")
                mm(ps[:, 0, 0:T], w2s[:], tlw[:])
                E.step("lora", mm(ps[:, 0, T:2 * T], a2s[:], tla[:]))
                fill(3)
                after(V, "silu")
                after(A, "sqq")
                for t in range(NT):
                    o = ps[:, 1, 8 * t:8 * t + 8]
                    mm(o[:, 0:2], sq[:, 0, cols(t)], headsel[:])
                    mm(o[:, 2:3], sq[:, 1, cols(t)], ones[:])
                    mm(o[:, 3:4], sq[:, 2, cols(t)], ones[:])
                    last = mm(o[:, 4:6], prod[:, cols(t)], headsel[:])
                E.step("norms", last)
                fill(2)
                after(V, "rkx")
                after(G, "ub")
                for t in range(NT):
                    mm(ps[:, 3, cols(t)], ub[:, t, 1:2].to_broadcast([P, P]), cum_up[:])
                    mm(ps[:, 3, T + 2 * t:T + 2 * t + 1], cum_up[:], ub[:, t, 1:2])
                    mm(ps[:, 3, T + 2 * t + 1:T + 2 * t + 2], strict_lo[:], ub[:, t, 1:2])
                    mm(ps[:, 2, cols(t)], rn[:, t, 2:3].to_broadcast([P, P]), ident[:])
                    mm(ps[:, 2, T + t * P:T + (t + 1) * P], rn[:, t, 3:4].to_broadcast([P, P]), ident[:])
                    mm(ps[:, 0, cols(t)], rne[:, t, :], ident[:])
                    last = mm(ps[:, 0, T + t * P:T + (t + 1) * P], ub[:, t, 0:1].to_broadcast([P, P]), ident[:])
                E.step("rows", last)
                fill(2)
                after(V, "qde")
                after(A, "ah1")
                for t in range(NT):
                    nc.tensor.transpose(ps[:, 1, cols(t)], rkv[:, 2, cols(t)], ident[:])
                    nc.tensor.transpose(ps[:, 1, T + t * P:T + (t + 1) * P], qkv[:, 2, cols(t)], ident[:])
                    nc.tensor.transpose(ps[:, 2, cols(t)], bhk[:, 0, cols(t)], ident[:])
                    nc.tensor.transpose(ps[:, 2, T + t * P:T + (t + 1) * P], bhk[:, 1, cols(t)], ident[:])
                    last = nc.tensor.transpose(ps[:, 0, cols(t)], kn[:, cols(t)], ident[:])
                E.step("tok", last)
                fill(1)
                for i, (bank, who, name) in enumerate(((3, None, None), (1, A, "vb1"), (2, A, "bk"), (0, A, "kd1"))):
                    if who is not None:
                        after(who, name)
                    t, h = i // 2, i % 2
                    mm(ps[:, bank, 0:2 * P], bhk[:, 0, cols(t)], arh[:, h, :, cols(t)])
                    E.step(f"in{i}", mm(ps[:, bank, 2 * P:4 * P], bhk[:, 1, cols(t)], arh[:, h, :, cols(t)]))
                after(V, "t0")
                for i in range(4):
                    t, h = i // 2, i % 2
                    last = mm(ps[:, 3, i * P:(i + 1) * P], arh[:, h, 0, cols(t)], bhk[:, 0, cols(t)])
                E.step("nab", last)
                for t, bank in enumerate((1, 2)):
                    after(V, f"t{t + 1}")
                    mm(ps[:, bank, 0:2 * P], kn[:, cols(t)], kq[:, :, cols(t)])
                    E.step(f"g{t}", mm(ps[:, bank, 2 * P:3 * P], kq[:, 0, cols(t)], kn[:, cols(t)]))
                fill(2)
                for i in LV:
                    m = 2 << i
                    after(V, f"x{i - 1}" if i else "xi")
                    for p in range(6):
                        lt = tr[:, p, 0, :] if p < 4 else tg[:, p - 4, 0, :]
                        last = mm(ps[:, 2 + i % 2, 64 * p:64 * p + 64], lt, half1(xi[:, p, :], m, 0))
                    E.step(f"Y{i}", last)
                    fill(1)
                    if i == 0:
                        after(G, "xti")
                    after(V, f"y{i}")
                    for p in range(6):
                        if i < 4:
                            mm(ps[:, 0, 64 * p:64 * p + 64], xt_[:, p, :], half1(yb[i % 2][:, p, :], m, 0))
                        last = mm(ps[:, 1, 64 * p:64 * p + 64], yb[i % 2][:, p, :], half1(xt_[:, p, :], m, 1))
                    E.step(f"X{i}", last)
                for c in CN:
                    t, b = c // 2, c % 2
                    if c == 0:
                        after(V, "xt4")
                        after(G, "vp1")
                    else:
                        after(V, f"sg{c - 1}")
                        mm(ps[:, 0, 0:P], ar[:, 0, cols(t)], st[:], stop=False)
                        mm(ps[:, 1, 0:P], kq[:, 0, cols(t)], sg[:])
                    for h in range(2):
                        hc = slice(RH * h, RH * h + RH)
                        last = mm(ps[:, 0, hc], tr[:, 2 * t + h, 2, :], vp[b][:, t, hc], start=c == 0)
                    E.step(f"c1_{c}", last)
                    if c > 0:
                        fill(1)
                    after(A, f"r{c}")
                    if c > 0:
                        after(V, f"g{c}c")
                        after(A, f"o{c - 1}")
                    for h in range(2):
                        hc = slice(RH * h, RH * h + RH)
                        mm(ps[:, 2, hc], xt_[:, 2 * t + h, :], rhs[:, 0, hc])
                    E.step(f"c2_{c}", mm(ps[:, 3, 0:P], xt_[:, 4 + t, :], rhs[:, 1, :] if c else vb[:, 0, :]))
                    after(A, f"un{c}")
                    after(V, f"vn{c}")
                    if c < 3:
                        mm(ps[:, 0, P:2 * P], bkt[:, 1, t, :], vp[b][:, t, :], stop=False)
                        mm(ps[:, 0, P:2 * P], bkt[:, 0, t, :], un[b][:], start=False)
                        E.step(f"c3_{c}", mm(ps[:, 1, P:2 * P], kd[:, t, :], vn[b][:]))
                    if c > 0:
                        mm(ps[:, 2, P:2 * P], ar[:, 1, cols(t)], st[:], stop=False)
                        mm(ps[:, 3, P:2 * P], qde[:, cols(t)], sg[:], stop=False)
                    for h in range(2):
                        o = ps[:, 2, P + RH * h:P + RH * h + RH]
                        hc = slice(RH * h, RH * h + RH)
                        mm(o, tr[:, 2 * t + h, 1, :], un[b][:, hc], start=c == 0, stop=False)
                        mm(o, tr[:, 2 * t + h, 3, :], vp[b][:, t, hc], start=False)
                    E.step(f"c4_{c}", mm(ps[:, 3, P:2 * P], tg[:, t, 1, :], vn[b][:], start=c == 0))
                pe.wait_ge(gate_in, 16 * u + 16)
                for t in range(NT):
                    for k in range(2):
                        last = mm(ps[:, 0, cols(t)], tlg[:, k, cols(t)], g2s[:, k, :], start=k == 0, stop=k == 1)
                E.step("gate", last)
                fill(3)
                after(V, "mix")
                for t in range(NT):
                    last = nc.tensor.transpose(ps[:, 1, cols(t)], yy[:, t, :], ident[:])
                E.step("mT", last)

            def take_out(act, u, j, mixing):
                act.wait_ge(quantum_done, QL + QU * u + 8 * (j + 1))
                if mixing is not None:
                    who, name = ((E, "tr1"), (E, "tr2"), (V, "gb"))[j]
                    act.wait_ge(who.sem, who.after(name, mixing))
                for t in range(NT):
                    last = nc.scalar.activation(pu[:, t, j * PW:(j + 1) * PW], ps[:, 4 + 2 * (j % 2) + t, 0:PW],
                                                ACT.Copy)
                last.then_inc(pass_out, 1)

            def mix_act(act, u, more):
                q_at = [0]

                def fill(n):
                    if more:
                        for _ in range(n):
                            split_hi(act, u + 1, q_at[0])
                            if q_at[0] in (9, 17):
                                take_out(act, u + 1, q_at[0] // 8 - 1, u)
                            q_at[0] += 1

                def after(steps, name):
                    act.wait_ge(steps.sem, steps.after(name, u))

                def fn(name, o, i, f=ACT.Copy, **kw):
                    A.step(name, nc.scalar.activation(o, i, f, **kw))

                act.wait_ge(pass_out, pass_columns(u, 2))
                fn("gates", thg, pu[:, :, 2 * PW:3 * PW], ACT.Tanh, scale=0.5)
                fill(3)
                after(E, "tr1")
                after(G, "up")
                for i, x in enumerate("rkv"):
                    fn(f"u{x}", rkv[:, i, :], ps[:, i // 2, (i % 2) * T:(i % 2 + 1) * T],
                       scale=up[:, OMM + i:OMM + i + 1])
                after(E, "tr2")
                for i, x in enumerate("qkv"):
                    fn(f"c{x}", qkv[:, i, :], ps[:, 2 + i // 2, (i % 2) * T:(i % 2 + 1) * T],
                       scale=up[:, TAP[3] + i:TAP[3] + i + 1])
                fill(3)
                after(E, "lora")
                fn("tw", sig[:], ps[:, 0, 0:T], ACT.Tanh, scale=0.5, bias=up[:, HW0:HW0 + 1])
                fn("ta", al[:], ps[:, 0, T:2 * T], ACT.Tanh, scale=0.5, bias=up[:, HA0:HA0 + 1])
                after(V, "kx")
                fn("sqk", sq[:, 0, :], kk[:], ACT.Square)
                fn("tq", th[:].rearrange("p (a b) -> p a b", a=3), qkv[:], ACT.Tanh, scale=0.5)
                after(V, "cex")
                fn("wex", wex[:], wex[:], ACT.Exp, scale=-KAPPA)
                fn("winv", winv[:], cum[:], ACT.Exp, scale=KAPPA)
                fn("winc", winc[:], cum[:], ACT.Exp, scale=-KAPPA)
                after(V, "silu")
                fn("sqq", sq[:, 1:3, :], qkv[:, 0:2, :], ACT.Square)
                fill(4)
                after(E, "rows")
                if more:
                    load_lora(act, u + 1)
                fn("egr", egr[:], ps[:, 3, 0:T], ACT.Exp)
                fn("ege", ege[:].rearrange("p a b -> p (a b)"), ps[:, 3, T:T + 4], ACT.Exp)
                after(V, "dl1")
                fn("edt", dd[:, :, 0, :], dd[:, :, 0, :], ACT.Exp)
                fn("edl", dd[:, :, 1, :], dd[:, :, 1, :], ACT.Exp, scale=-1.0)
                after(V, "rr")
                for h in range(2):
                    hp = slice(RH * h, RH * h + RH)
                    fn(f"ah{h}", arh[hp, h, :, :], ar[hp, :, :])
                fill(1)
                after(E, "tok")
                fn("v", vt[:].rearrange("p a b -> p (a b)"), ps[:, 1, 0:T])
                after(G, "uh")
                for t in range(NT):
                    fn(f"vb{t}", vb[:, t, :], ps[:, 1, T + t * P:T + (t + 1) * P], scale=uh[:, t:t + 1])
                fn("bk", bkt[:].rearrange("p a t b -> p (a t b)"), ps[:, 2, :])
                for t in range(NT):
                    fn(f"kd{t}", kd[:, t, :], ps[:, 0, cols(t)], scale=ege[:, t, 1:2])
                fill(2)
                for i in LV:
                    fill(1)
                for c in CN:
                    t, b = c // 2, c % 2
                    rb = slice(CH * b, CH * b + CH)
                    if c > 0:
                        fill(1)
                    after(E, f"c1_{c}")
                    fn(f"r{c}", rhs[:, 0, :], ps[:, 0, 0:P])
                    after(E, f"c2_{c}")
                    fn(f"un{c}", un[b][rb, :], ps[rb, 2, 0:P], scale=-1.0)
                    after(E, f"c4_{c}")
                    fn(f"y{c}", yy[rb, t, :], ps[rb, 2, P:2 * P])
                    fn(f"o{c}", oo[rb, t, :], ps[rb, 3, P:2 * P])
                fill(3)
                after(V, "yc")
                fn("ysq", sq[:, 0, :], yy[:].rearrange("p a b -> p (a b)"), ACT.Square)
                after(A, "o3")
                fn("osq", sq[:, 1, :], oo[:].rearrange("p a b -> p (a b)"), ACT.Square)
                if more:
                    after(E, "gate")
                    load_gate(act, u + 1)
                after(E, "mT")
                fn("mT", mixT[:, bass.ds(u, 1), :], ps[:, 1:2, 0:T])
                if more:
                    load_ln(act, u + 1)
                    take_out(act, u + 1, 2, u)

            def mix_dve(dve, u, more):
                q_at = [0]

                def fill(n):
                    if more:
                        for _ in range(n):
                            split_lo(dve, u + 1, q_at[0])
                            q_at[0] += 1

                def after(steps, name):
                    dve.wait_ge(steps.sem, steps.after(name, u))

                def done(name):
                    after(V, name)

                def tt(name, o, x, y, op=ALU.mult):
                    V.step(name, nc.vector.tensor_tensor(o, x, y, op))

                def ts(name, o, x, s1, s2, op0, op1=ALU.bypass):
                    if s2 is None:
                        V.step(name, nc.vector.tensor_scalar(o, x, s1, None, op0))
                    else:
                        V.step(name, nc.vector.tensor_scalar(o, x, s1, s2, op0, op1))

                def stv(name, o, x, s, y, op0=ALU.mult, op1=ALU.add):
                    V.step(name, nc.vector.scalar_tensor_tensor(o, x, s, y, op0, op1))

                after(A, "gates")
                ts("ga", ga[:], thg[:, :, P:2 * P], 0.5, 0.5, ALU.mult, ALU.add)
                stv("gz", gb[:], thg[:, :, 0:P], 1.0, pu[:, :, 2 * PW:2 * PW + P], ALU.add, ALU.mult)
                done("gz")
                stv("gb", gb[:], thg[:, :, 2 * P:3 * P], 1.0, gb[:], ALU.add, ALU.mult)
                fill(3)
                after(A, "uv")
                for i, x in enumerate("rkv"):
                    stv(f"s{x}", rkv[:, i, 1:T], ps[:, i // 2, (i % 2) * T:(i % 2 + 1) * T - 1],
                        up[:, MIX_R + i:MIX_R + i + 1], rkv[:, i, 1:T])
                after(A, "cv")
                for j in range(3):
                    d = 3 - j
                    for i, x in enumerate("qkv"):
                        if j:
                            done(f"c{j - 1}{x}")
                        stv(f"c{j}{x}", qkv[:, i, d:T], ps[:, 2 + i // 2, (i % 2) * T:(i % 2 + 1) * T - d],
                            up[:, TAP[j] + i:TAP[j] + i + 1], qkv[:, i, d:T])
                done("sv")
                ts("kx", kk[:], rkv[:, 1, :], up[:, K_K:K_K + 1], None, ALU.mult)
                fill(3)
                after(A, "ta")
                ts("sig", sig[:], sig[:], 0.5, 0.5, ALU.mult, ALU.add)
                ts("al", al[:], al[:], 0.5, 0.5, ALU.mult, ALU.add)
                done("sig")
                V.step("cum", nc.vector.tensor_tensor_scan(cum[:], restart[:], sig[:], 0.0, ALU.mult, ALU.add))
                done("cum")
                tt("cex", wex[:], cum[:], sig[:], ALU.subtract)
                ts("kf", kmod[:], al[:], up[:, K_A:K_A + 1], up[:, OKA:OKA + 1], ALU.mult, ALU.add)
                done("kf")
                tt("kmod", kmod[:], kmod[:], rkv[:, 1, :])
                ts("rr0", prod[:], rkv[:, 0, :], up[:, R_K:R_K + 1], None, ALU.mult)
                done("rr0")
                tt("pr", prod[:], prod[:], kmod[:])
                after(A, "tq")
                stv("silu", qkv[:], th[:].rearrange("p (a b) -> p a b", a=3), 1.0, qkv[:], ALU.add, ALU.mult)
                fill(2)
                after(E, "norms")
                sums = ps[:, 1, 0:16].rearrange("p (t c) -> p t c", t=NT)
                tt("nrm", nrm[:], sums[:, :, 0:4], eps4[:].unsqueeze(1).to_broadcast([P, NT, 4]), ALU.add)
                V.step("bon", nc.vector.tensor_copy(bon[:], sums[:, :, 4:6]))
                done("nrm")
                rsqrt(nc, dve, V, "n", u, rn[:], nrm[:], rtmp[:])
                ts("rq", rn[:, :, 2:3], rn[:, :, 2:3], P ** -0.5, None, ALU.mult)
                V.step("rkx", nc.vector.tensor_copy(rne[:].rearrange("p t (h j) -> p t h j", h=2),
                                                    rn[:, :, 0:2].unsqueeze(3).to_broadcast([P, NT, 2, RH])))
                fill(2)
                after(A, "ege")
                V.step("gcc", nc.vector.tensor_copy(gcc[:], ps[:, 3, T:T + 4:2]))
                done("gcc")
                for t in range(NT):
                    ts(f"dt{t}", dd[:, t, 0, :], ps[:, 3, cols(t)], gcc[:, t:t + 1], 0.0, ALU.subtract, ALU.min)
                    ts(f"dl{t}", dd[:, t, 1, :], ps[:, 3, cols(t)], gcc[:, t:t + 1], 0.0, ALU.subtract, ALU.max)
                ts("nege", nege[:], ege[:, :, 0], -1.0, None, ALU.mult)
                tt("kk", kk[:], kk[:], ps[:, 0, 0:T])
                tt("kn", kn[:], qkv[:, 1, :], ps[:, 2, T:2 * T])
                tt("qn", kq[:, 1, :], qkv[:, 0, :], ps[:, 2, 0:T])
                done("kn")
                tt("kb", kq[:, 0, :], kn[:], ps[:, 0, T:2 * T])
                after(A, "winc")
                tt("aw", al[:], al[:], winv[:])
                done("kk")
                tt("ap", ar[:, 0, :], kk[:], wex[:])
                tt("rr", ar[:, 1, :], rkv[:, 0, :], winc[:])
                done("aw")
                tt("bh", bhk[:, 0, :], al[:], kk[:])
                tt("kh", bhk[:, 1, :], kmod[:], winv[:])
                done("qn")
                tt("qde", qde[:], kq[:, 1, :], egr[:])
                fill(1)
                for i, bank in enumerate((3, 1, 2, 0)):
                    after(E, f"in{i}")
                    tt(f"t{i}", tr[:, i, :, :], ps[:, bank, :].rearrange("p (a b) -> p a b", a=4), m4[:])
                after(E, "nab")
                tt("nab", low[:, 0:4, :], ps[:, 3, :].rearrange("p (a b) -> p a b", a=4),
                   strict_lo[:].unsqueeze(1).to_broadcast([P, 4, P]))
                after(G, "dml")
                for t, bank in enumerate((1, 2)):
                    after(E, f"g{t}")
                    tt(f"g{t}", tg[:, t, :, :], ps[:, bank, 0:2 * P].rearrange("p (a b) -> p a b", a=2),
                       dm[:, t, 0:2, :])
                    tt(f"l{t}", low[:, 4 + t, :], ps[:, bank, 2 * P:3 * P], dm[:, t, 2, :])
                fill(2)
                done("l1")
                tt("xm", xi[:], low[:], lev[:, 0:1, :].to_broadcast([P, 6, P]))
                done("xm")
                tt("xi", xi[:], ident[:].unsqueeze(1).to_broadcast([P, 6, P]), xi[:], ALU.subtract)
                for i in LV:
                    m = 2 << i
                    nb = P // (2 * m)

                    def compact(bank):
                        return ps[:, bank, 0:6 * 64].rearrange("p (a b j) -> p a b j", a=6, j=m)

                    after(E, f"Y{i}")
                    if i < 2:
                        after(G, "zb")
                    else:
                        after(G, f"z{i - 2}")
                    tt(f"y{i}", half(yb[i % 2][:], m, 0), compact(2 + i % 2),
                       half1(lev[:, i + 1, :], m, 0).unsqueeze(1).to_broadcast([P, 6, nb, m]))
                    fill(1)
                    after(E, f"X{i}")
                    if i < 4:
                        tt(f"x{i}", half(xi[:], m, 0), half(xi[:], m, 0), compact(0), ALU.subtract)
                    tt(f"xt{i}", half(xt_[:], m, 1), half(xt_[:], m, 1), compact(1), ALU.subtract)
                for c in CN:
                    t, b = c // 2, c % 2
                    rb = slice(CH * b, CH * b + CH)
                    wc = winc[:, CH * c + CH - 1:CH * c + CH]
                    gl = egr[:, CH * c + CH - 1:CH * c + CH]
                    if c > 0:
                        fill(1)
                        after(E, f"c1_{c}")
                        stv(f"g{c}c", rhs[:, 1, :], ps[:, 1, 0:P], nege[:, t:t + 1], vb[:, t, :])
                        if c < 3:
                            done(f"s{c - 1}b")
                            ts(f"sw{c}", stw[:], st[:], wc, None, ALU.mult)
                    after(E, f"c2_{c}")
                    V.step(f"vn{c}", nc.vector.tensor_copy(vn[b][rb, :], ps[rb, 3, 0:P]))
                    if c < 3:
                        if c > 0:
                            after(E, f"c4_{c}")
                            done(f"sw{c}")
                        else:
                            after(E, "c3_0")
                        for h in range(2):
                            hp = slice(RH * h, RH * h + RH)
                            o = ps[hp, 0, P + RH * h:P + RH * h + RH]
                            if c == 0:
                                ts(f"s0{'ab'[h]}", st[hp, hp], o, wc[hp], None, ALU.mult)
                            else:
                                stv(f"s{c}{'ab'[h]}", st[hp, hp], o, wc[hp], stw[hp, hp])
                        if c == 0:
                            V.step("sg0", nc.vector.tensor_copy(sg[:], ps[:, 1, P:2 * P]))
                        else:
                            stv(f"sg{c}", sg[:], sg[:], gl, ps[:, 1, P:2 * P])
                fill(3)
                after(A, "o3")
                y4 = yy[:].rearrange("p t (h j) -> p (t h) j", h=2)
                V.step("ys", nc.vector.tensor_reduce(ym[:], y4, AX.X, ALU.add))
                done("ys")
                ts("nm", ym[:], ym[:], 1.0 / RH, None, ALU.mult)
                done("nm")
                tt("yc", y4, y4, ym[:].unsqueeze(2).to_broadcast([P, 4, RH]), ALU.subtract)
                after(A, "osq")
                V.step("yv", nc.vector.tensor_reduce(stt[:, 0:4], sq[:, 0, :].rearrange("p (a j) -> p a j", j=RH),
                                                     AX.X, ALU.add))
                V.step("ov", nc.vector.tensor_reduce(stt[:, 4:6], sq[:, 1, :].rearrange("p (a j) -> p a j", j=P),
                                                     AX.X, ALU.add))
                done("ov")
                tt("st1", stt[:], stt[:], st_scale[:])
                done("st1")
                tt("st2", stt[:], stt[:], st_eps[:], ALU.add)
                done("st2")
                rsqrt(nc, dve, V, "r", u, rs[:], stt[:], rst[:])
                tt("yn", y4, y4, rs[:, 0:4].unsqueeze(2).to_broadcast([P, 4, RH]))
                dve.wait_ge(ln_in, 32 * u + 32)
                done("yn")
                tt("ylw", yy[:], yy[:], lnw[:].unsqueeze(1).to_broadcast([P, NT, P]))
                after(G, "bvb")
                done("ylw")
                tt("ybv", yy[:], yy[:], bv[:], ALU.add)
                after(E, "gate")
                done("ybv")
                tt("yg", yy[:], yy[:], ps[:, 0, 0:T].rearrange("p (a b) -> p a b", a=NT))
                done("yg")
                tt("yga", yy[:], yy[:], ga[:])
                after(G, "ogb")
                done("yga")
                tt("mix", yy[:], yy[:], oo[:], ALU.add)

            def mix_pool(pool, u, more):
                def after(steps, name):
                    pool.wait_ge(steps.sem, steps.after(name, u))

                def tt(name, o, x, y, op=ALU.mult):
                    G.step(name, nc.gpsimd.tensor_tensor(o, x, y, op))

                def clear(name, tile):
                    eye = ident[:].unsqueeze(1).to_broadcast([P, 6, P])
                    tt(name, tile[:], eye, eye, ALU.subtract)

                after(E, "tr1")
                clear("za", yb[0])
                clear("zb", yb[1])
                tt("up", up[:].unsqueeze(2), par[:, :, bass.ds(u, 1)], ones[:].unsqueeze(1).to_broadcast([P, NPAR, 1]))
                for t in range(NT):
                    last = nc.gpsimd.tensor_tensor(ub[:, t, :].unsqueeze(2), bg[:, t, :, bass.ds(u, 1)],
                                                   ones[:].unsqueeze(1).to_broadcast([P, 2, 1]), ALU.mult)
                G.step("ub", last)
                after(G, "ub")
                tt("uh", uh[:], ub[:, :, 0], halves[:].to_broadcast([P, NT]))
                after(A, "edl")
                for t in range(NT):
                    tt(f"dm{t}", dm[:, t, 0:2, :], dd[:, t, 0:1, :].to_broadcast([P, 2, P]), m4[:, 0:2, :])
                tt("dml", dm[:, :, 2, :], dd[:, :, 1, :], strict_lo[:].unsqueeze(1).to_broadcast([P, NT, P]))
                after(A, "v")
                for b in range(2):
                    rb = slice(CH * b, CH * b + CH)
                    after(G, ("dml", "vp0")[b])
                    tt(f"vp{b}", vp[b][rb, :, :], vt[rb, :, :], ones[rb, :].unsqueeze(1).to_broadcast([CH, NT, P]))
                after(G, "vp1")
                after(V, "bon")
                tt("bv", bv[:].rearrange("p t (h j) -> p t h j", h=2), vt[:].rearrange("p t (h j) -> p t h j", h=2),
                   bon[:].unsqueeze(3).to_broadcast([P, NT, 2, RH]))
                pool.wait_ge(ln_in, 32 * u + 32)
                after(G, "bv")
                tt("bvb", bv[:], bv[:], lnb[:].unsqueeze(1).to_broadcast([P, NT, P]), ALU.add)
                after(V, "l1")
                lt1 = lev[:, 6:7, :]
                tt("xtm", xt_[:, 0:4, :], tr[:, :, 0, :], lt1.to_broadcast([P, 4, P]))
                tt("xtg", xt_[:, 4:6, :], tg[:, :, 0, :], lt1.to_broadcast([P, 2, P]))
                after(G, "xtg")
                tt("xti", xt_[:], ident[:].unsqueeze(1).to_broadcast([P, 6, P]), xt_[:], ALU.subtract)
                for i in range(3):
                    after(E, f"X{i}")
                    clear(f"z{i}", yb[i % 2])
                after(V, "r10")
                tt("on", oo[:], oo[:], rs[:, 4:6].unsqueeze(2).to_broadcast([P, NT, P]))
                after(G, "on")
                tt("onw", oo[:], oo[:], gnw[:].unsqueeze(1).to_broadcast([P, NT, P]))
                after(G, "onw")
                tt("ogb", oo[:], oo[:], gb[:])

            with nc.Block() as block:
                @block.sync
                def _(sp):
                    load_unit_weights(sp, 0)
                    with sp.Fori(1, NU) as u:
                        load_unit_weights(sp, u)

                @block.gpsimd
                def _(pool):
                    for tile in (arh, vp[0], vp[1], un[0], un[1], vn[0], vn[1], st):
                        nc.gpsimd.memset(tile[:], 0.0)
                    with pool.Fori(0, NU - 1) as u:
                        mix_pool(pool, u, True)
                    mix_pool(pool, NU - 1, False)

                @block.scalar
                def _(act):
                    for q in range(QU):
                        split_hi(act, 0, q)
                        if q in (9, 17):
                            take_out(act, 0, q // 8 - 1, None)
                    take_out(act, 0, 2, None)
                    with act.Fori(0, NU - 1) as u:
                        mix_act(act, u, True)
                    mix_act(act, NU - 1, False)

                @block.vector
                def _(dve):
                    for q in range(QU):
                        split_lo(dve, 0, q)
                    with dve.Fori(0, NU - 1) as u:
                        mix_dve(dve, u, True)
                    mix_dve(dve, NU - 1, False)

                @block.tensor
                def _(pe):
                    for q in range(QU):
                        project(pe, 0, q)
                    with pe.Fori(0, NU - 1) as u:
                        mix_pe(pe, u, True)
                    mix_pe(pe, NU - 1, False)
        mix_ctx.close()

        CB = 512
        NB = D // CB
        wr = sb("wr", [P, 4, 4, CB])
        whi = [sb(f"whi{i}", [P, 2, CB], F32R) for i in range(2)]
        wlo = [sb(f"wlo{i}", [P, 2, CB], F32R) for i in range(2)]
        row = sb("row", [P, D])
        ssy = sb("ssy", [P, NT, NB])
        ssx = sb("ssx", [P, NT])
        rr = sb("rr", [P, NT])
        rtm = sb("rtm", [P, NT])
        x2 = keep[:].rearrange("p a b -> p (a b)").rearrange("p (t n) -> p t n", t=NT)

        class Stream:

            def __init__(self, tag):
                self.landed = [sem(f"{tag}_in{i}") for i in range(4)]
                self.hi, self.lo, self.used = sem(f"{tag}_hi"), sem(f"{tag}_lo"), sem(f"{tag}_used")

        def stage_hi(act, s, n, src):
            if not (isinstance(n, int) and n < 2):
                act.wait_ge(s.used, n - 1)
            nc.scalar.activation(whi[s.par][:], src, ACT.Copy).then_inc(s.hi, 1)
            s.par ^= 1

        def stage_lo(dve, s, n, src):
            dve.wait_ge(s.hi, n + 1)
            nc.vector.tensor_tensor(wlo[s.par][:], src, whi[s.par][:].bitcast(F32), ALU.subtract).then_inc(s.lo, 1)
            s.par ^= 1

        def stage_mm(pe, s, n, left_hi, left_lo, o, first, last):
            pe.wait_ge(s.lo, n + 1)
            for k in range(2):
                for t in range(NT):
                    xs = slice(t * P, (t + 1) * P)
                    nc.tensor.matmul(o(t), left_hi[:, k, xs], whi[s.par][:, k, :], start=first and k == 0, stop=False,
                                     skip_group_check=True)
                    nc.tensor.matmul(o(t), left_hi[:, k, xs], wlo[s.par][:, k, :], start=False, stop=False,
                                     skip_group_check=True)
                    mm = nc.tensor.matmul(o(t), left_lo[:, k, xs], whi[s.par][:, k, :], start=False,
                                          stop=last and k == 1, skip_group_check=True)
            mm.then_inc(s.used, 1)
            s.par ^= 1

        post_act = [f"sq{i}" for i in range(2 * NB)]
        post_dve = ["sum", "var"] + rsqrt_names("p") + ["n0", "n1", "a0", "a1"]

        def post_norm_act(act, A, junk, used, n):
            act.wait_ge(used, n)
            for t in range(NT):
                for b in range(NB):
                    if t + b:
                        act.wait_ge(A.sem, A.after(f"sq{t * NB + b - 1}"))
                    A.step(f"sq{t * NB + b}", nc.scalar.activation(junk, ps[:, 2 * b + t, :], ACT.Square,
                                                                   accum_out=ssy[:, t, b:b + 1]))

        def post_norm_dve(dve, A, V, y, base, dst):
            def done(name):
                dve.wait_ge(V.sem, V.after(name))

            dve.wait_ge(A.sem, A.after(f"sq{2 * NB - 1}"))
            V.step("sum", nc.vector.tensor_reduce(ssx[:], ssy[:], AX.X, ALU.add))
            done("sum")
            V.step("var", nc.vector.tensor_scalar(ssx[:], ssx[:], 1.0 / D, NORM_EPS, ALU.mult, ALU.add))
            done("var")
            rsqrt(nc, dve, V, "p", 0, rr[:], ssx[:], rtm[:])
            for t in range(NT):
                banks = ps[:].rearrange("p (n t) c -> p n t c", t=NT)[:, :, t, :]
                V.step(f"n{t}", nc.vector.scalar_tensor_tensor(
                    y[:, t, :].rearrange("p (n c) -> p n c", c=CB), banks, rr[:, t:t + 1],
                    row[:].rearrange("p (n c) -> p n c", c=CB), ALU.mult, ALU.mult))
            for t in range(NT):
                done(f"n{t}")
                V.step(f"a{t}", nc.vector.tensor_tensor(dst[:, t, :], y[:, t, :], base[:, t, :], ALU.add))

        with ExitStack() as c3:
            x1 = sb("x1", [P, NT, D], F32, c3)
            y1 = sb("y1", [P, NT, D], F32, c3)
            junk = sb("junk3", [P, D], F32, c3)
            S = Stream("out")
            x1_in, row_in = sem("x1_in"), sem("row_in")
            A = Steps(sem("out_act"), ["xh"] + post_act + ["ss0", "ss1", "xs0", "xs1"] + [f"hi{g}" for g in G8])
            V = Steps(sem("out_dve"), ["xl"] + post_dve + ["v2"] + rsqrt_names("q") + [f"lo{g}" for g in G8])
            E = Steps(sem("out_pe"), [f"x{g}" for g in G8])
            w3 = a["w_out"][0].rearrange("(kc p) n -> p kc n", p=P)
            QB = KC // 2

            def quantum(q):
                return wr[:, (q // 2) % 4, 2 * (q % 2):2 * (q % 2) + 2, :]

            with nc.Block() as block:
                @block.sync
                def _(sp):
                    def load(b, i):
                        sp.dma_start(wr[:, i, :, :], w3[:, 4 * i:4 * i + 4, bass.ds(b * CB, CB)]
                                     ).then_inc(S.landed[i], 16)

                    for i in range(4):
                        load(0, i)
                    sp.dma_start(x1[:], a["x"][0].rearrange("(t p) n -> p t n", p=P)).then_inc(x1_in, 16)
                    sp.dma_start(row[:], a["norm_mix_post"][0].partition_broadcast(P)).then_inc(row_in, 16)
                    with sp.Fori(1, NB) as b:
                        for i in range(4):
                            sp.wait_ge(S.lo, b * QB + 2 * i + 2 - QB)
                            load(b, i)

                @block.scalar
                def _(act):
                    S.par = 0
                    A.step("xh", nc.scalar.activation(xh[:], keep[:], ACT.Copy))

                    def block_hi(b):
                        for q in range(QB):
                            if q % 2 == 0:
                                act.wait_ge(S.landed[q // 2], b * 16 + 16)
                            stage_hi(act, S, b * QB + q, quantum(q))

                    block_hi(0)
                    with act.Fori(1, NB) as b:
                        block_hi(b)
                    post_norm_act(act, A, junk[:, 0:CB], S.used, NB * QB)
                    for t in range(NT):
                        act.wait_ge(V.sem, V.after(f"a{t}"))
                        if t:
                            act.wait_ge(A.sem, A.after("ss0"))
                        A.step(f"ss{t}", nc.scalar.activation(junk[:], x2[:, t, :], ACT.Square,
                                                              accum_out=ssx[:, t:t + 1]))
                    act.wait_ge(V.sem, V.after("q10"))
                    for t in range(NT):
                        A.step(f"xs{t}", nc.scalar.activation(y1[:, t, :], x2[:, t, :], ACT.Copy,
                                                              scale=rr[:, t:t + 1]))
                    transpose_x_act(act, A, E, NORM2)

                @block.vector
                def _(dve):
                    S.par = 0
                    dve.wait_ge(A.sem, A.after("xh"))
                    V.step("xl", nc.vector.tensor_tensor(xl[:], keep[:], xh[:].bitcast(F32), ALU.subtract))

                    def block_lo(b):
                        for q in range(QB):
                            stage_lo(dve, S, b * QB + q, quantum(q))

                    with dve.Fori(0, NB) as b:
                        block_lo(b)
                    dve.wait_ge(x1_in, 16)
                    dve.wait_ge(row_in, 16)
                    post_norm_dve(dve, A, V, y1[:], x1[:], x2)
                    dve.wait_ge(A.sem, A.after("ss1"))
                    V.step("v2", nc.vector.tensor_scalar(ssx[:], ssx[:], 1.0 / D, NORM_EPS, ALU.mult, ALU.add))
                    dve.wait_ge(V.sem, V.after("v2"))
                    rsqrt(nc, dve, V, "q", 0, rr[:], ssx[:], rtm[:])
                    transpose_x_dve(dve, V, A, NORM2)

                @block.tensor
                def _(pe):
                    S.par = 0
                    pe.wait_ge(V.sem, V.after("xl"))
                    with pe.Fori(0, NB) as b:
                        for q in range(QB):
                            stage_mm(pe, S, b * QB + q, xh[:, 2 * q:2 * q + 2, :], xl[:, 2 * q:2 * q + 2, :],
                                     lambda t: ps[:, bass.ds(b * NT + t, 1), :], q == 0, q == QB - 1)
                    pe.wait_ge(A.sem, A.after("xs1"))
                    transpose_x_pe(pe, E, y1, V)

        hidT = sb("hidT", [P, FKC, T])
        hh = [sb(f"hh{i}", [P, 2, T], F32R) for i in range(2)]
        hl = [sb(f"hl{i}", [P, 2, T], F32R) for i in range(2)]
        tg_ = sb("ffn_tanh", [P, NT, CB])
        gg = sb("ffn_gate", [P, NT, CB])
        hid = sb("ffn_hidden", [P, NT, CB])
        y2 = sb("y2", [P, NT, D])
        S = Stream("ffn")
        row2_in, result_out = sem("row2_in"), sem("result_out")
        tanh_done, gate_done, hidden_done = sem("tanh_done"), sem("gate_done"), sem("hidden_done")
        turned, stored = sem("turned"), sem("stored")
        down_in = [sem(f"down_in{i}") for i in range(2)]
        left_hi, left_lo = sem("left_hi"), sem("left_lo")
        A = Steps(sem("ffn_act"), post_act)
        V = Steps(sem("ffn_dve"), post_dve)
        wg = a["ffn_w_gate"][0].rearrange("(kc p) n -> p kc n", p=P)
        wu = a["ffn_w_up"][0].rearrange("(kc p) n -> p kc n", p=P)
        wd = a["ffn_w_down"][0].rearrange("(j k p) n -> j p k n", k=2, p=P)
        QF = 2 * (KC // 2)
        QD = QF * FB
        JD = FKC // 2

        def quantum(q):
            return wr[:, (q // 2) % 4, 2 * (q % 2):2 * (q % 2) + 2, :]

        def down_quantum(s, b):
            return wr[:, 2 * s:2 * s + 2, :, :].rearrange("p k a c -> p k (a c)")[:, :, b * CB:(b + 1) * CB]

        with nc.Block() as block:
            @block.sync
            def _(sp):
                def load(jb, f, first):
                    if not (first and f < 4):
                        sp.wait_ge(S.lo, jb * QF + 2 * f - 6)
                    w = wg if f < 4 else wu
                    kc = 4 * (f % 4)
                    sp.dma_start(wr[:, f % 4, :, :], w[:, kc:kc + 4, bass.ds(jb * CB, CB)]
                                 ).then_inc(S.landed[f % 4], 16)

                for f in range(8):
                    load(0, f, True)
                sp.dma_start(row[:], a["norm_ffn_post"][0].partition_broadcast(P)).then_inc(row2_in, 16)
                with sp.Fori(1, FB) as jb:
                    for f in range(8):
                        load(jb, f, False)

                def load_down(j, s, split):
                    sp.wait_ge(S.lo, split)
                    src = wd[j] if isinstance(j, int) else wd[bass.ds(j, 1)].rearrange("o p k n -> p (o k) n")
                    sp.dma_start(wr[:, 2 * s:2 * s + 2, :, :].rearrange("p k a c -> p k (a c)"), src
                                 ).then_inc(down_in[s], 16)

                load_down(0, 0, QD - 4)
                load_down(1, 1, QD)
                with sp.Fori(1, JD // 2) as jj:
                    for s in range(2):
                        load_down(jj * 2 + s, s, jj * (2 * NB) + (QD + (s + 1) * NB - 2 * NB))
                sp.wait_ge(V.sem, V.after("a1"))
                sp.dma_start(out[0].rearrange("(t p) n -> p t n", p=P), y2[:]).then_inc(result_out, 16)
                sp.wait_ge(result_out, 16)

            @block.scalar
            def _(act):
                S.par = 0

                def store(jb):
                    act.wait_ge(turned, jb + 1)
                    nc.scalar.activation(hidT[:, bass.ds(jb * 4, 4), :],
                                         ps[:, 4:6, :].rearrange("p a (k c) -> p (a k) c", c=T), ACT.Copy
                                         ).then_inc(stored, 1)

                def block_act(jb, first):
                    for q in range(QF):
                        if q % 2 == 0:
                            act.wait_ge(S.landed[(q // 2) % 4], jb * 32 + 16 * (q // 8 + 1))
                        stage_hi(act, S, jb * QF + q, quantum(q))
                        if q == 3 and not first:
                            store(jb - 1)
                        if q == 9:
                            act.wait_ge(S.used, jb * QF + QF // 2)
                            nc.scalar.activation(tg_[:], ps[:, 0:2, :], ACT.Tanh, scale=0.5).then_inc(tanh_done, 1)

                block_act(0, True)
                with act.Fori(1, FB) as jb:
                    block_act(jb, False)
                store(FB - 1)

                def down_act(j, s, n, landed):
                    if not isinstance(j, int):
                        act.wait_ge(S.used, n - NB)
                    nc.scalar.activation(hh[s][:], hidT[:, bass.ds(j * 2, 2), :], ACT.Copy).then_inc(left_hi, 1)
                    act.wait_ge(down_in[s], landed)
                    for b in range(NB):
                        stage_hi(act, S, n + b, down_quantum(s, b))

                act.wait_ge(stored, FB)
                for s in range(2):
                    down_act(s, s, QD + NB * s, 16)
                with act.Fori(1, JD // 2) as jj:
                    for s in range(2):
                        down_act(jj * 2 + s, s, jj * (2 * NB) + (QD + NB * s), jj * 16 + 16)
                post_norm_act(act, A, tg_[:, 0, :], S.used, QD + NB * JD)

            @block.vector
            def _(dve):
                S.par = 0

                def hidden(jb):
                    dve.wait_ge(S.used, jb * QF + QF)
                    nc.vector.scalar_tensor_tensor(hid[:], gg[:], 0.5, ps[:, 2:4, :], ALU.mult, ALU.mult
                                                   ).then_inc(hidden_done, 1)

                def block_dve(jb, first):
                    for q in range(QF):
                        stage_lo(dve, S, jb * QF + q, quantum(q))
                        if q == 1 and not first:
                            dve.wait_ge(gate_done, jb)
                            hidden(jb - 1)
                        if q == 9:
                            dve.wait_ge(tanh_done, jb + 1)
                            nc.vector.scalar_tensor_tensor(gg[:], tg_[:], 1.0, ps[:, 0:2, :], ALU.add, ALU.mult
                                                           ).then_inc(gate_done, 1)

                block_dve(0, True)
                with dve.Fori(1, FB) as jb:
                    block_dve(jb, False)
                dve.wait_ge(gate_done, FB)
                hidden(FB - 1)

                def down_dve(j, s, n):
                    dve.wait_ge(left_hi, j + 1)
                    nc.vector.tensor_tensor(hl[s][:], hidT[:, bass.ds(j * 2, 2), :], hh[s][:].bitcast(F32),
                                            ALU.subtract).then_inc(left_lo, 1)
                    for b in range(NB):
                        stage_lo(dve, S, n + b, down_quantum(s, b))

                for s in range(2):
                    down_dve(s, s, QD + NB * s)
                with dve.Fori(1, JD // 2) as jj:
                    for s in range(2):
                        down_dve(jj * 2 + s, s, jj * (2 * NB) + (QD + NB * s))
                dve.wait_ge(row2_in, 16)
                post_norm_dve(dve, A, V, y2[:], x2, y2[:])

            @block.tensor
            def _(pe):
                S.par = 0

                def turn(jb):
                    pe.wait_ge(hidden_done, jb + 1)
                    for k in range(4):
                        for t in range(NT):
                            c0 = (k % 2) * T + t * P
                            last = nc.tensor.transpose(ps[:, 4 + k // 2, c0:c0 + P], hid[:, t, k * P:(k + 1) * P],
                                                       ident[:])
                    last.then_inc(turned, 1)

                def block_pe(jb, first):
                    for q in range(QF):
                        g = q // (QF // 2)
                        if q == 0 and not first:
                            pe.wait_ge(gate_done, jb)
                        if q == 2 and not first:
                            turn(jb - 1)
                        kc = 2 * (q % (QF // 2))
                        stage_mm(pe, S, jb * QF + q, xh[:, kc:kc + 2, :], xl[:, kc:kc + 2, :],
                                 lambda t: ps[:, 2 * g + t, :], kc == 0, kc == KC - 2)

                block_pe(0, True)
                with pe.Fori(1, FB) as jb:
                    block_pe(jb, False)
                turn(FB - 1)
                pe.wait_ge(stored, FB)

                def down_pe(j, s, n, first, last):
                    pe.wait_ge(left_lo, j + 1)
                    for b in range(NB):
                        stage_mm(pe, S, n + b, hh[s][:], hl[s][:], lambda t: ps[:, 2 * b + t, :], first, last)

                for s in range(2):
                    down_pe(s, s, QD + NB * s, s == 0, False)
                with pe.Fori(1, JD // 2) as jj:
                    for s in range(2):
                        down_pe(jj * 2 + s, s, jj * (2 * NB) + (QD + NB * s), False, False)


_INS = ["x", "norm_mix_pre", "norm_mix_post", "norm_ffn_pre", "norm_ffn_post", "w_in", "rwkv_mix", "rwkv_w0",
        "rwkv_w2", "rwkv_a0", "rwkv_a2", "rwkv_g2", "rwkv_k_k", "rwkv_k_a", "rwkv_r_k", "rwkv_ln_w", "rwkv_ln_b",
        "gdn_conv_w", "gdn_a_log", "gdn_dt_bias", "gdn_norm_w", "w_out", "ffn_w_gate", "ffn_w_up", "ffn_w_down"]


def kernel(**inputs):
    import concourse.bacc as bacc
    from concourse.bass_utils import run_bass_kernel_spmd

    nc = bacc.Bacc("TRN2", target_bir_lowering=False, num_devices=1)
    arrays, aps = {}, {}
    for name in _INS:
        v = np.ascontiguousarray(inputs[name])
        arrays[f"in_{name}"] = v
        aps[name] = nc.dram_tensor(f"in_{name}", v.shape, mybir.dt.from_np(v.dtype), kind="ExternalInput").ap()
    out = nc.dram_tensor("out_x", (1, T, D), F32, kind="ExternalOutput").ap()
    build(nc, aps, out)
    r = run_bass_kernel_spmd(nc, [arrays], core_ids=[0])
    return r.results[0]["out_x"]
```

```python
from contextlib import ExitStack
import math

import numpy as np
import concourse.bass as bass
from concourse import mybir

F32 = mybir.dt.float32
F32R = mybir.dt.float32r
I32 = mybir.dt.int32
ALU = mybir.AluOpType
ACT = mybir.ActivationFunctionType
AX = mybir.AxisListType

P = 128
D = 2048
T = 256
NT = T // P
KC = D // P
NU = D // P
CH = 64
RH = 64
FF = 5632
FB = FF // 512
FKC = FF // P
LORA_W, LORA_A, LORA_G = 96, 96, 256
COL_LORA = 3 * D
COL_QKV = 3 * D + LORA_W + LORA_A + LORA_G
COL_Z = COL_QKV + 3 * D
COL_BETA = COL_Z + D
COL_GATE = COL_BETA + 32
NORM_EPS = 1e-6
GN_EPS = 64e-5
KAPPA = math.exp(-0.5)

PW = 384
QU = 24
QL = 16
QBUF = 4
LEAD = 2
FIRST = 18

(MIX_R, MIX_K, MIX_V, W0, A0, K_K, K_A, R_K) = range(8)
TAP = (8, 11, 16, 19)
NORM1, NORM2 = 14, 15
OMM, OKA, HW0, HA0 = 22, 25, 26, 27
NPAR = 28


class Steps:

    def __init__(self, sem, names):
        self.sem, self.names, self.n, self.next = sem, list(names), len(names), 0
        assert len(set(names)) == len(names)

    def at(self, name):
        assert self.names[self.next] == name, (name, self.names[self.next])
        self.next = (self.next + 1) % self.n
        return 1

    def after(self, name, unit=0, lag=0):
        return unit * self.n + (self.names.index(name) + 1 - lag * self.n)


    def step(self, name, ins):
        ins.then_inc(self.sem, self.at(name))


def rsqrt_names(tag):
    return [f"{tag}{i}" for i in range(11)]


def rsqrt(nc, dve, done, tag, unit, y, v, t, lag=0):
    names = iter(rsqrt_names(tag))

    def step(ins):
        name = next(names)
        done.step(name, ins)
        dve.wait_ge(done.sem, done.after(name, unit, lag))

    step(nc.vector.tensor_scalar(y.bitcast(I32), v.bitcast(I32), -0.5, 1597463007.0, ALU.mult, ALU.add))
    step(nc.vector.tensor_scalar(v, v, -0.5, None, ALU.mult))
    for _ in range(3):
        step(nc.vector.tensor_tensor(t, y, y, ALU.mult))
        step(nc.vector.tensor_tensor(t, t, v, ALU.mult))
        step(nc.vector.scalar_tensor_tensor(y, t, 1.5, y, ALU.add, ALU.mult))


def build(nc, a, out):
    with ExitStack() as ctx:
        def sb(name, shape, dt=F32, c=ctx):
            return c.enter_context(nc.sbuf_tensor(name, shape, dt))

        def sem(name):
            return ctx.enter_context(nc.semaphore(name))

        ps = ctx.enter_context(nc.psum_tensor("ps", [P, 8, 512], F32))
        xh = sb("xh", [P, KC, T], F32R)
        xl = sb("xl", [P, KC, T], F32R)
        ident = sb("ident", [P, P])
        par = sb("par", [P, NPAR, NU])
        par2 = par[:].rearrange("p a b -> p (a b)")
        keep = sb("keep", [P, KC, T])
        mixT = keep

        weights_in = [sem(f"weights_in{i}") for i in range(3)]
        small_in = sem("small_in")
        x_in = sem("x_in")
        masks_made = sem("masks_made")
        hi_ready, lo_ready = sem("hi_ready"), sem("lo_ready")
        quantum_done, pass_out = sem("quantum_done"), sem("pass_out")
        front_sem = [sem(f"{e}_front") for e in ("pe", "act", "dve", "pool")]
        back_sem = [sem(f"{e}_back") for e in ("pe", "act", "dve", "pool")]
        lora_in, gate_in, lnw_in, lnb_in = sem("lora_in"), sem("gate_in"), sem("lnw_in"), sem("lnb_in")

        w_in3 = a["w_in"][0].rearrange("(kc p) n -> p kc n", p=P)

        mix_ctx = ctx.enter_context(ExitStack())

        def mb(name, shape, dt=F32):
            return sb(name, shape, dt, mix_ctx)

        raw = [mb(f"raw{i}", [P, 8, PW]) for i in range(3)]
        pu = mb("pu", [P, NT, 3 * PW])
        hi = [mb(f"hi{i}", [P, 2, PW], F32R) for i in range(QBUF)]
        lo = [mb(f"lo{i}", [P, 2, PW], F32R) for i in range(QBUF)]
        tlw = mb("tlw", [LORA_W, T])
        tla = mb("tla", [LORA_A, T])
        tlg = mb("tlg", [P, 2, T])
        bg = mb("bg", [P, NT, 2, NU])
        up_masks = mb("up_masks", [P, 2, P])
        strict_up = up_masks[:, 0, :]
        cum_up = up_masks[:, 1, :]
        strict_lo = mb("strict_lo", [P, P])
        lev = mb("lev", [P, 7, P])
        ones = mb("ones", [P, 1])
        halves = mb("halves", [P, 1])
        headsel = mb("headsel", [P, 2])
        eps4 = mb("eps4", [P, 4])
        st_scale = mb("st_scale", [P, 6])
        st_eps = mb("st_eps", [P, 6])
        restart = mb("restart", [P, T])
        gnw = mb("gnw", [P, P])

        def columns(j, u):
            if j == 0:
                return [u * P, D + u * P, 2 * D + u * P]
            if j == 1:
                return [COL_QKV + u * P, COL_QKV + D + u * P, COL_QKV + 2 * D + u * P]
            return [COL_Z + u * P, COL_GATE + u * P, COL_GATE + D + u * P]

        def load_unit_weights(sp, u):
            for i in range(6):
                j, half = i // 2, i % 2
                fill = 4 + i
                sp.wait_ge(lo_ready, 24 * u + (4 * fill - 8))
                for seg, col in enumerate(columns(j, u)):
                    sp.dma_start(raw[fill % 3][:, :, seg * P:(seg + 1) * P],
                                 w_in3[:, 8 * half:8 * half + 8, bass.ds(col, P)]
                                 ).then_inc(weights_in[fill % 3], 16)

        def count(u, q):
            return q if u is None else QU * u + (QL + q)

        def raw_quantum(u, q, w):
            return raw[(q // 4 + (u is not None)) % 3][:, 2 * (q % 4):2 * (q % 4) + 2, 0:w]

        def split_hi(act, u, q, w=PW):
            fill = q // 4 + (0 if u is None else 4)
            arrived = 48 * (fill // 3 + 1)
            act.wait_ge(weights_in[fill % 3], arrived if u is None else 96 * u + arrived)
            if not (u is None and q < QBUF):
                act.wait_ge(quantum_done, count(u, q + 1 - QBUF))
            nc.scalar.activation(hi[q % QBUF][:, :, 0:w], raw_quantum(u, q, w), ACT.Copy).then_inc(hi_ready, 1)

        def split_lo(dve, u, q, w=PW):
            dve.wait_ge(hi_ready, count(u, q + 1))
            nc.vector.tensor_tensor(lo[q % QBUF][:, :, 0:w], raw_quantum(u, q, w),
                                    hi[q % QBUF][:, :, 0:w].bitcast(F32), ALU.subtract).then_inc(lo_ready, 1)

        def project(pe, u, q, w=PW):
            j = q // 8
            if q % 8 == 0 and u is not None:
                pe.wait_ge(pass_out, 3 * u + (2 + j))
            pe.wait_ge(lo_ready, count(u, q + 1))
            for k in range(2):
                kc = 2 * (q % 8) + k
                for t in range(NT):
                    o = ps[:, (4 + 2 * j if u is None else 6) + t, 0:w]
                    xs = slice(t * P, (t + 1) * P)
                    nc.tensor.matmul(o, xh[:, kc, xs], hi[q % QBUF][:, k, 0:w], start=kc == 0, stop=False)
                    nc.tensor.matmul(o, xh[:, kc, xs], lo[q % QBUF][:, k, 0:w], start=False, stop=False)
                    last = nc.tensor.matmul(o, xl[:, kc, xs], hi[q % QBUF][:, k, 0:w],
                                            start=False, stop=kc == KC - 1)
            last.then_inc(quantum_done, 1)

        def take_out(act, u, j):
            act.wait_ge(quantum_done, count(u, 8 * (j + 1)))
            for t in range(NT):
                last = nc.scalar.activation(pu[:, t, (j % 3) * PW:(j % 3 + 1) * PW], ps[:, 6 + t, 0:PW], ACT.Copy)
            last.then_inc(pass_out, 1)

        def pass_columns(u, j):
            return 3 * u + (3 + j)

        G8 = range(KC // 2)
        pre_dve = Steps(sem("pre_dve"), ["var"] + rsqrt_names("rs") + ["par"] + [f"lo{g}" for g in G8]
                        + ["omm", "oka", "hw0", "ha0", "lomm0", "lomm1", "lomm2", "lomm3", "gnw"]
                        + ["shift0", "shift1", "shift2", "shift3", "tlg", "beta", "y", "ymax", "yabs", "sp", "g"])
        pre_act = Steps(sem("pre_act"), ["ss0", "ss1", "xs0", "xs1"] + [f"hi{g}" for g in G8]
                        + ["un0", "un1", "un2", "un3", "tlw", "tla", "tlg", "beta", "alog", "exp", "ln"])
        pre_pe = Steps(sem("pre_pe"), ["par"] + [f"x{g}" for g in G8] + ["lora"])

        def transpose_x_pe(pe, done, src, read_out):
            for g in G8:
                if g >= 4:
                    pe.wait_ge(read_out.sem, read_out.after(f"lo{g - 4}"))
                for k in range(2):
                    for t in range(NT):
                        last = nc.tensor.transpose(ps[:, g % 4, k * T + t * P:k * T + (t + 1) * P],
                                                   src[:, t, (2 * g + k) * P:(2 * g + k + 1) * P], ident[:])
                done.step(f"x{g}", last)

        def transpose_x_act(act, done, turned, weight):
            for g in G8:
                act.wait_ge(turned.sem, turned.after(f"x{g}"))
                for k in range(2):
                    kc = 2 * g + k
                    last = nc.scalar.activation(xh[:, kc, :], ps[:, g % 4, k * T:(k + 1) * T], ACT.Copy,
                                                scale=par[:, weight, kc:kc + 1])
                done.step(f"hi{g}", last)

        def transpose_x_dve(dve, done, high, weight):
            for g in G8:
                dve.wait_ge(high.sem, high.after(f"hi{g}"))
                for k in range(2):
                    kc = 2 * g + k
                    last = nc.vector.scalar_tensor_tensor(
                        xl[:, kc, :], ps[:, g % 4, k * T:(k + 1) * T], par[:, weight, kc:kc + 1],
                        xh[:, kc, :].bitcast(F32), ALU.mult, ALU.subtract)
                done.step(f"lo{g}", last)

        w2s = mb("w2s", [LORA_W, P])
        a2s = mb("a2s", [LORA_A, P])
        g2s = mb("g2s", [P, 2, P])
        lnw = mb("lnw", [P, P])
        lnb = mb("lnb", [P, P])

        def load_lora(eng, u):
            eng.dma_start(w2s[:], a["rwkv_w2"][0][:, bass.ds(u * P, P)]).then_inc(lora_in, 16)
            eng.dma_start(a2s[:], a["rwkv_a2"][0][:, bass.ds(u * P, P)]).then_inc(lora_in, 16)

        def load_gate(eng, u):
            g2 = a["rwkv_g2"][0].rearrange("(k p) n -> p k n", p=P)
            eng.dma_start(g2s[:], g2[:, :, bass.ds(u * P, P)]).then_inc(gate_in, 16)

        def load_lnw(eng, u):
            eng.dma_start(lnw[:], a["rwkv_ln_w"][0][bass.ds(u * P, P)].partition_broadcast(P)).then_inc(lnw_in, 16)

        def load_lnb(eng, u):
            eng.dma_start(lnb[:], a["rwkv_ln_b"][0][bass.ds(u * P, P)].partition_broadcast(P)).then_inc(lnb_in, 16)

        N_SMALL = 21
        with ExitStack() as c1:
            def tb(name, shape, dt=F32):
                return sb(name, shape, dt, c1)

            xt = tb("xt", [P, NT, D])
            junk = tb("junk", [P, D])
            prow = [tb(f"prow{i}", [P, P]) for i in range(3)]
            ss = tb("ss", [P, NT])
            rx = tb("rx", [P, NT])
            rt = tb("rt", [P, NT])
            lp = tb("lp", [P, NT, 480])
            lmix = tb("lmix", [P, 4])
            lomm = tb("lomm", [P, 4])
            lf = tb("lf", [P, 4, T])
            alog = tb("alog", [P, NU])
            dtb = tb("dtb", [P, NU])
            sp1 = tb("sp1", [P, NT, NU])
            sp2 = tb("sp2", [P, NT, NU])
            lora_cols = ((0, LORA_W), (LORA_W, LORA_A), (LORA_W + LORA_A, P), (LORA_W + LORA_A + P, P))

            with nc.Block() as block:
                @block.sync
                def _(sp):
                    sp.dma_start(xt[:], a["x"][0].rearrange("(t p) n -> p t n", p=P)).then_inc(x_in, 16)

                    def rows(v):
                        return v.rearrange("(u p) -> u p", p=P)

                    mix = a["rwkv_mix"][0]
                    vecs = [mix[0:D], mix[D:2 * D], mix[2 * D:3 * D], a["rwkv_w0"][0], a["rwkv_a0"][0],
                            a["rwkv_k_k"][0], a["rwkv_k_a"][0], a["rwkv_r_k"][0].rearrange("h n -> (h n)")]
                    for i, v in enumerate(vecs):
                        sp.dma_start(prow[0][16 * i:16 * i + 16, :], rows(v)).then_inc(small_in, 16)
                    conv = a["gdn_conv_w"][0]
                    for i in range(2):
                        sp.dma_start(prow[1][48 * i:48 * i + 48, :], rows(conv[i])).then_inc(small_in, 16)
                        sp.dma_start(prow[2][48 * i:48 * i + 48, :], rows(conv[2 + i])).then_inc(small_in, 16)
                    sp.dma_start(prow[1][96:112, :], rows(a["norm_mix_pre"][0])).then_inc(small_in, 16)
                    sp.dma_start(prow[1][112:128, :], rows(a["norm_ffn_pre"][0])).then_inc(small_in, 16)
                    with nc.allow_non_contiguous_dma(reason="a few hundred single values"):
                        for i, (c0, n) in enumerate(lora_cols):
                            sp.dma_start(lmix[0:n, i:i + 1],
                                         mix[3 * D + c0:3 * D + c0 + n].rearrange("(p a) -> p a", a=1)
                                         ).then_inc(small_in, 16)
                    sp.dma_start(alog[:], a["gdn_a_log"][0].partition_broadcast(P)).then_inc(small_in, 16)
                    sp.dma_start(dtb[:], a["gdn_dt_bias"][0].partition_broadcast(P)).then_inc(small_in, 16)
                    sp.dma_start(gnw[:], a["gdn_norm_w"][0].partition_broadcast(P)).then_inc(small_in, 16)
                    load_lora(sp, 0)
                    load_gate(sp, 0)
                    load_lnw(sp, 0)
                    load_lnb(sp, 0)
                    for fill in range(4):
                        j, half = fill // 2, fill % 2
                        if fill >= 3:
                            sp.wait_ge(lo_ready, 4 * fill - 8)
                        segs = ([(0, COL_LORA, P), (P, COL_LORA + P, P), (2 * P, COL_LORA + 2 * P, P)] if j == 0
                                else [(0, COL_LORA + PW, 64), (64, COL_BETA, 16), (80, COL_BETA + 16, 16)])
                        for at, col, n in segs:
                            sp.dma_start(raw[fill % 3][:, :, at:at + n],
                                         w_in3[:, 8 * half:8 * half + 8, col:col + n]
                                         ).then_inc(weights_in[fill % 3], 16)

                @block.gpsimd
                def _(pool):
                    made = [0]

                    def chain(ins):
                        made[0] += 1
                        ins.then_inc(masks_made, 1)
                        pool.wait_ge(masks_made, made[0])

                    def keep(tile, pattern, base, cm, op=ALU.is_ge, fill=0.0):
                        chain(nc.gpsimd.affine_select(out=tile, in_=tile, compare_op=op, fill=fill, base=base,
                                                      pattern=pattern, channel_multiplier=cm))

                    def chunks(tile):
                        return tile.rearrange("p (b j) -> p b j", j=CH)

                    chain(nc.gpsimd.memset(ident[:], 0.0))
                    keep(ident[:], [[-1, P]], 0, 1, ALU.not_equal, 1.0)
                    for tile, base in ((cum_up, 0), (strict_up, -1)):
                        chain(nc.gpsimd.memset(tile, 1.0))
                        keep(chunks(tile), [[CH, 2], [1, CH]], base, -1)
                        keep(chunks(tile), [[-CH, 2], [0, CH]], 0, 1)
                    chain(nc.gpsimd.memset(strict_lo[:], 1.0))
                    keep(chunks(strict_lo[:]), [[-CH, 2], [-1, CH]], -1, 1)
                    keep(chunks(strict_lo[:]), [[CH, 2], [0, CH]], CH - 1, -1)
                    for i in range(6):
                        m = 1 << i
                        nb = P // (2 * m)
                        v = lev[:, i, :].rearrange("p (b e j) -> p b e j", e=2, j=m)
                        chain(nc.gpsimd.memset(lev[:, i, :], 0.0))
                        chain(nc.gpsimd.memset(v[:, :, 0, :], 1.0))
                        keep(v[:, :, 0, :], [[-2 * m, nb], [0, m]], -m, 1)
                        keep(v[:, :, 0, :], [[2 * m, nb], [0, m]], 2 * m - 1, -1)
                    v = lev[:, 6, :].rearrange("p (b e) -> p b e", e=2)
                    chain(nc.gpsimd.memset(lev[:, 6, :], 0.0))
                    keep(v[:, :, 1], [[-2, P // 2]], 0, 1, ALU.not_equal, 1.0)
                    chain(nc.gpsimd.memset(ones[:], 1.0))
                    chain(nc.gpsimd.memset(halves[:], 0.5))
                    chain(nc.gpsimd.memset(headsel[:], 1.0))
                    keep(headsel[:, 0:1], [[0, 1]], RH - 1, -1)
                    keep(headsel[:, 1:2], [[0, 1]], -RH, 1)
                    chain(nc.gpsimd.memset(restart[:], 1.0))
                    chain(nc.gpsimd.memset(restart[:].rearrange("p (c j) -> p c j", j=CH)[:, :, 0:1], 0.0))
                    nc.gpsimd.memset(eps4[:, 0:2], 1e-6)
                    nc.gpsimd.memset(eps4[:, 2:4], 4e-6)
                    nc.gpsimd.memset(st_scale[:, 0:4], 1.0 / RH)
                    nc.gpsimd.memset(st_scale[:, 4:6], 1.0 / P)
                    nc.gpsimd.memset(st_eps[:, 0:4], GN_EPS)
                    nc.gpsimd.memset(st_eps[:, 4:6], NORM_EPS)

                @block.scalar
                def _(act):
                    A, D_, Pe = pre_act, pre_dve, pre_pe
                    act.wait_ge(x_in, 16)
                    for t in range(NT):
                        if t:
                            act.wait_ge(A.sem, A.after("ss0"))
                        A.step(f"ss{t}", nc.scalar.activation(junk[:], xt[:, t, :], ACT.Square,
                                                              accum_out=ss[:, t:t + 1]))
                    act.wait_ge(D_.sem, D_.after("rs10"))
                    for t in range(NT):
                        A.step(f"xs{t}", nc.scalar.activation(xt[:, t, :], xt[:, t, :], ACT.Copy,
                                                              scale=rx[:, t:t + 1]))
                    act.wait_ge(D_.sem, D_.after("par"))
                    transpose_x_act(act, A, Pe, NORM1)
                    for q in range(QL):
                        split_hi(act, None, q, PW if q < 8 else 96)
                    for j, w in ((0, PW), (1, 96)):
                        act.wait_ge(quantum_done, 8 * (j + 1))
                        for t in range(NT):
                            last = nc.scalar.activation(lp[:, t, PW * j:PW * j + w], ps[:, 4 + 2 * j + t, 0:w],
                                                        ACT.Copy)
                        last.then_inc(pass_out, 1)
                    act.wait_ge(Pe.sem, Pe.after("lora"))
                    act.wait_ge(D_.sem, D_.after("lomm3"))
                    for i, (_, n) in enumerate(lora_cols):
                        A.step(f"un{i}", nc.scalar.activation(
                            lf[0:n, i, :], ps[0:n, i // 2, (i % 2) * T:(i % 2 + 1) * T], ACT.Copy,
                            scale=lomm[0:n, i:i + 1]))
                    act.wait_ge(D_.sem, D_.after("shift3"))
                    A.step("tlw", nc.scalar.activation(tlw[:], lf[0:LORA_W, 0, :], ACT.Tanh))
                    A.step("tla", nc.scalar.activation(tla[:], lf[0:LORA_A, 1, :], ACT.Copy))
                    A.step("tlg", nc.scalar.activation(tlg[:], lf[:, 2:4, :], ACT.Tanh, scale=0.5))
                    act.wait_ge(pass_out, 2)
                    A.step("beta", nc.scalar.activation(bg[:, :, 0, :], lp[:, :, 448:464], ACT.Tanh, scale=0.5))
                    A.step("alog", nc.scalar.activation(alog[:], alog[:], ACT.Exp))
                    act.wait_ge(D_.sem, D_.after("yabs"))
                    A.step("exp", nc.scalar.activation(sp1[:], sp1[:], ACT.Exp))
                    act.wait_ge(A.sem, A.after("exp"))
                    A.step("ln", nc.scalar.activation(sp1[:], sp1[:], ACT.Ln, bias=1.0))

                @block.vector
                def _(dve):
                    A, D_, Pe = pre_act, pre_dve, pre_pe

                    def step(name, ins):
                        D_.step(name, ins)
                        dve.wait_ge(D_.sem, D_.after(name))

                    dve.wait_ge(A.sem, A.after("ss1"))
                    step("var", nc.vector.tensor_scalar(ss[:], ss[:], 1.0 / D, NORM_EPS, ALU.mult, ALU.add))
                    rsqrt(nc, dve, D_, "rs", 0, rx[:], ss[:], rt[:])
                    dve.wait_ge(Pe.sem, Pe.after("par"))
                    step("par", nc.vector.tensor_copy(par2[:, 0:352], ps[:, 0, 0:352]))
                    transpose_x_dve(dve, D_, A, NORM1)
                    for name, src, dst, num, f0, f1 in (("omm", MIX_R, OMM, 3, -1.0, 1.0), ("oka", K_A, OKA, 1, -1.0, 1.0),
                                                        ("hw0", W0, HW0, 1, 0.5, 0.0), ("ha0", A0, HA0, 1, 0.5, 0.0)):
                        step(name, nc.vector.tensor_scalar(par[:, dst:dst + num, :], par[:, src:src + num, :], f0, f1,
                                                           ALU.mult, ALU.add))
                    dve.wait_ge(small_in, 16 * N_SMALL)
                    for i, (_, n) in enumerate(lora_cols):
                        step(f"lomm{i}", nc.vector.tensor_scalar(lomm[0:n, i:i + 1], lmix[0:n, i:i + 1], -1.0, 1.0,
                                                                 ALU.mult, ALU.add))
                    step("gnw", nc.vector.tensor_scalar(gnw[:], gnw[:], 0.25, None, ALU.mult))
                    for q in range(QL):
                        split_lo(dve, None, q, PW if q < 8 else 96)
                    dve.wait_ge(A.sem, A.after("un3"))
                    for i, (_, n) in enumerate(lora_cols):
                        src = ps[0:n, i // 2, (i % 2) * T:(i % 2 + 1) * T]
                        step(f"shift{i}", nc.vector.scalar_tensor_tensor(
                            lf[0:n, i, 1:T], src[:, 0:T - 1], lmix[0:n, i:i + 1], lf[0:n, i, 1:T],
                            ALU.mult, ALU.add))
                    dve.wait_ge(A.sem, A.after("beta"))
                    step("tlg", nc.vector.tensor_scalar(tlg[:], tlg[:], 0.5, 0.5, ALU.mult, ALU.add))
                    step("beta", nc.vector.tensor_scalar(bg[:, :, 0, :], bg[:, :, 0, :], 0.5, 0.5, ALU.mult, ALU.add))
                    step("y", nc.vector.tensor_tensor(sp2[:], lp[:, :, 464:480],
                                                      dtb[:].unsqueeze(1).to_broadcast([P, NT, NU]), ALU.add))
                    step("ymax", nc.vector.tensor_scalar(sp1[:], sp2[:], 0.0, -2.0, ALU.max, ALU.mult))
                    step("yabs", nc.vector.tensor_tensor(sp1[:], sp1[:], sp2[:], ALU.add))
                    dve.wait_ge(A.sem, A.after("ln"))
                    step("sp", nc.vector.scalar_tensor_tensor(sp2[:], sp2[:], 0.0, sp1[:], ALU.max, ALU.add))
                    step("g", nc.vector.scalar_tensor_tensor(
                        bg[:, :, 1, :], sp2[:], -1.0, alog[:].unsqueeze(1).to_broadcast([P, NT, NU]),
                        ALU.mult, ALU.mult))

                @block.tensor
                def _(pe):
                    A, D_, Pe = pre_act, pre_dve, pre_pe
                    pe.wait_ge(masks_made, 2)
                    pe.wait_ge(small_in, 16 * N_SMALL)
                    for i, nr in enumerate((P, P, 96)):
                        last = nc.tensor.transpose(ps[:, 0, P * i:P * i + nr], prow[i][0:nr, :], ident[0:nr, 0:nr])
                    Pe.step("par", last)
                    pe.wait_ge(D_.sem, D_.after("par"))
                    pe.wait_ge(A.sem, A.after("xs1"))
                    transpose_x_pe(pe, Pe, xt, D_)
                    pe.wait_ge(D_.sem, D_.after("lo7"))
                    for q in range(QL):
                        project(pe, None, q, PW if q < 8 else 96)
                    pe.wait_ge(pass_out, 2)
                    for i, (c0, n) in enumerate(lora_cols):
                        for t in range(NT):
                            last = nc.tensor.transpose(
                                ps[0:n, i // 2, (i % 2) * T + t * P:(i % 2) * T + (t + 1) * P],
                                lp[:, t, c0:c0 + n], ident[:])
                    Pe.step("lora", last)

        with ExitStack() as c2:
            def tb(name, shape, dt=F32):
                return sb(name, shape, dt, c2)

            up = tb("up", [P, NPAR])
            ub = tb("ub", [P, NT, 2])
            uh = tb("uh", [P, NT])
            th = tb("th", [P, 3 * T])
            thg = th[:].rearrange("p (t c) -> p t c", t=NT)
            rkv = tb("rkv", [P, 3, T])
            qkv = tb("qkv", [P, 3, T])
            sq = tb("sq", [P, 3, T])
            sig = tb("sig", [P, T])
            cum = tb("cum", [P, T])
            wex = tb("wex", [P, T])
            winc = tb("winc", [P, T])
            winv = tb("winv", [P, T])
            al = tb("al", [P, T])
            kk = tb("kk", [P, T])
            kmod = tb("kmod", [P, T])
            prod = tb("prod", [P, T])
            ar = tb("ar", [P, 2, T])
            arh = tb("arh", [P, 2, 2, T])
            bhk = tb("bhk", [P, 2, T])
            kn = tb("kn", [P, T])
            kq = tb("kq", [P, 2, T])
            qde = tb("qde", [P, T])
            egr = tb("egr", [P, T])
            nrm = tb("nrm", [P, NT, 4])
            rn = tb("rn", [P, NT, 4])
            rtmp = tb("rtmp", [P, NT, 4])
            bon = tb("bon", [P, NT, 2])
            rne = sig[:].rearrange("p (t c) -> p t c", t=NT)
            gcc = tb("gcc", [P, NT])
            ege = tb("ege", [P, NT, 2])
            nege = tb("nege", [P, NT])
            wlast = tb("wlast", [P, T // CH])
            glast = tb("glast", [P, T // CH])
            dd = tb("dd", [P, NT, 2, P])
            sqo = dd[:].rearrange("p a b c -> p a (b c)")
            dm = sq[:].rearrange("p a (b c) -> p (a b) c", b=2).rearrange("p (t k) c -> p t k c", t=NT)
            vt = prod[:].rearrange("p (t c) -> p t c", t=NT)
            vp = [tb(f"vp{b}", [P, NT, P]) for b in range(2)]
            vb = tb("vb", [P, NT, P])
            bkt = tb("bkt", [P, 2, NT, P])
            kd = tb("kd", [P, NT, P])
            tr = tb("tr", [P, 4, 4, P])
            tg = tb("tg", [P, NT, 2, P])
            xi = tb("xi", [P, 6, P])
            xt_ = tb("xit", [P, 6, P])
            yb = [tb(f"yb{i}", [P, 6, P]) for i in range(2)]
            rhs = tb("rhs", [P, 2, P])
            un = [tb(f"un{b}", [P, P]) for b in range(2)]
            vn = [tb(f"vn{b}", [P, P]) for b in range(2)]
            st = tb("st", [P, P])
            stw = tb("stw", [P, P])
            sg = tb("sg", [P, P])
            yy = tb("yy", [P, NT, P])
            oo = tb("oo", [P, NT, P])
            ga = tb("ga", [P, NT, P])
            gb = tb("gb", [P, NT, P])
            bv = tb("bv", [P, NT, P])
            ym = tb("ym", [P, 4])
            stt = tb("stt", [P, 6])
            rs = tb("rs", [P, 6])
            rst = tb("rst", [P, 6])

            LV = range(5)
            CN = range(T // CH)
            pe_names = (["tr1", "tr2", "lora", "norms", "rows", "tok", "in0", "in1", "in2", "in3", "nab", "g0", "g1"]
                        + [f"{x}{i}" for i in LV for x in "YX"])
            act_names = ["ur", "uk", "uv", "cq", "ck", "cv", "tw", "ta", "sqk", "tq", "wex", "winv", "winc",
                         "sqq", "egr", "ege", "edt", "edl", "ah0", "ah1", "v", "vb0", "vb1", "bk", "kd0", "kd1",
                         "gates"]
            dve_names = (["sr", "sk", "sv"] + [f"c{j}{x}" for j in range(3) for x in "qkv"]
                         + ["kx", "sig", "al", "cum", "cex", "kf", "kmod", "rr0", "pr", "silu", "nrm", "bon"]
                         + rsqrt_names("n") + ["rq", "rkx", "gcc", "dt0", "dl0", "dt1", "dl1", "kk", "kn", "qn",
                                               "aw", "kh", "nege", "wlast", "glast", "kb", "ap", "rr", "bh", "qde",
                                               "t0", "t1", "t2", "t3", "nab", "g0", "l0", "g1", "l1", "xm", "xi"]
                         + [f"{x}{i}" for i in LV for x in ("y", "x", "xt") if not (x == "x" and i == 4)]
                         + ["ga", "gz", "gb"])
            pool_names = ["up", "za", "zb", "ub", "uh", "dm0", "dm1", "dml", "vp0", "vp1",
                          "xtm", "xtg", "xti", "z0", "z1", "z2", "bv", "bvb"]
            pe_back = [f"c{k}_{c}" for c in CN for k in (1, 2, 3, 4) if not (k == 3 and c == 3)] + ["gate", "mT"]
            act_back = [f"{x}{c}" for c in CN for x in ("r", "un", "y", "o")] + ["ysq", "osq", "mT"]
            dve_back = (["vn0", "s0a", "s0b", "sg0", "g1c", "sw1", "vn1", "s1a", "s1b", "sg1",
                         "g2c", "sw2", "vn2", "s2a", "s2b", "sg2", "g3c", "vn3"]
                        + ["ys", "nm", "yc", "yv", "ov", "st1", "st2"] + rsqrt_names("r")
                        + ["yn", "ylw", "ybv", "yg", "yga", "mix"])
            E, A, V, G = (Steps(m, names) for m, names in zip(front_sem, (pe_names, act_names, dve_names, pool_names)))
            EB, AB, VB, GB = (Steps(m, names) for m, names in
                              zip(back_sem, (pe_back, act_back, dve_back, ["on", "onw", "ogb"])))

            def wait(eng, steps, name, u, lag=0):
                eng.wait_ge(steps.sem, steps.after(name, u, lag))

            def cols(t):
                return slice(t * P, (t + 1) * P)

            def half(tile, m, odd):
                return tile.rearrange("p a (b e j) -> p a b e j", e=2, j=m)[:, :, :, odd, :]

            def half1(tile, m, odd):
                return tile.rearrange("p (b e j) -> p b e j", e=2, j=m)[:, :, odd, :]

            def mm(o, l, r, start=True, stop=True):
                return nc.tensor.matmul(o, l, r, start=start, stop=stop, skip_group_check=True)

            def chunk_pe(pe, u, lag, k, c):
                def after(steps, name):
                    wait(pe, steps, name, u, lag)

                t, b = c // 2, c % 2
                heads = [(h, slice(RH * h, RH * h + RH)) for h in range(2)]
                if k == 1:
                    if c == 0:
                        after(V, "xt4")
                        after(G, "vp1")
                    else:
                        after(VB, f"sg{c - 1}")
                        after(AB, f"o{c - 1}")
                        mm(ps[:, 4, 0:P], ar[:, 0, cols(t)], st[:], stop=False)
                        mm(ps[:, 5, 0:P], kq[:, 0, cols(t)], sg[:])
                    for h, hc in heads:
                        last = mm(ps[:, 4, hc], tr[:, 2 * t + h, 2, :], vp[b][:, t, hc], start=c == 0)
                    EB.step(f"c1_{c}", last)
                elif k == 2:
                    after(AB, f"r{c}")
                    if c > 0:
                        after(VB, f"g{c}c")
                    for h, hc in heads:
                        mm(ps[:, 4, P + RH * h:P + RH * h + RH], xt_[:, 2 * t + h, :], rhs[:, 0, hc])
                    EB.step(f"c2_{c}", mm(ps[:, 5, P:2 * P], xt_[:, 4 + t, :], rhs[:, 1, :] if c else vb[:, 0, :]))
                else:
                    after(AB, f"un{c}")
                    after(VB, f"vn{c}")
                    if c < 3:
                        mm(ps[:, 5, 2 * P:3 * P], bkt[:, 1, t, :], vp[b][:, t, :], stop=False)
                        mm(ps[:, 5, 2 * P:3 * P], bkt[:, 0, t, :], un[b][:], start=False)
                        EB.step(f"c3_{c}", mm(ps[:, 5, 3 * P:4 * P], kd[:, t, :], vn[b][:]))
                    if c > 0:
                        mm(ps[:, 4, 2 * P:3 * P], ar[:, 1, cols(t)], st[:], stop=False)
                    for h, hc in heads:
                        o = ps[:, 4, 2 * P + RH * h:2 * P + RH * h + RH]
                        mm(o, tr[:, 2 * t + h, 1, :], un[b][:, hc], start=c == 0, stop=False)
                        mm(o, tr[:, 2 * t + h, 3, :], vp[b][:, t, hc], start=False)
                    if c > 0:
                        mm(ps[:, 4, 3 * P:4 * P], qde[:, cols(t)], sg[:], stop=False)
                    EB.step(f"c4_{c}", mm(ps[:, 4, 3 * P:4 * P], tg[:, t, 1, :], vn[b][:], start=c == 0))

            def gate_pe(pe, u, lag):
                pe.wait_ge(gate_in, 16 * u + (16 - 16 * lag))
                for t in range(NT):
                    for k in range(2):
                        last = mm(ps[:, 5, cols(t)], tlg[:, k, cols(t)], g2s[:, k, :], start=k == 0, stop=k == 1)
                EB.step("gate", last)

            def turn_pe(pe, u, lag):
                wait(pe, VB, "mix", u, lag)
                for t in range(NT):
                    last = nc.tensor.transpose(ps[:, 4, cols(t)], yy[:, t, :], ident[:])
                EB.step("mT", last)

            def mix_pe(pe, u, prev, more):
                q_at = [FIRST]

                def fill(n):
                    for _ in range(n):
                        if more or q_at[0] < QU:
                            project(pe, u, q_at[0])
                            q_at[0] += 1

                def chunk(k, c):
                    if prev:
                        chunk_pe(pe, u, 1, k, c)

                def after(steps, name):
                    wait(pe, steps, name, u)

                pe.wait_ge(pass_out, pass_columns(u, 1))
                if prev:
                    wait(pe, V, "xt4", u, 1)
                for i in range(3):
                    for t in range(NT):
                        last = nc.tensor.transpose(ps[:, i // 2, (i % 2) * T + t * P:(i % 2) * T + (t + 1) * P],
                                                   pu[:, t, i * P:(i + 1) * P], ident[:])
                E.step("tr1", last)
                for i in range(3):
                    for t in range(NT):
                        last = nc.tensor.transpose(ps[:, 2 + i // 2, (i % 2) * T + t * P:(i % 2) * T + (t + 1) * P],
                                                   pu[:, t, PW + i * P:PW + (i + 1) * P], ident[:])
                E.step("tr2", last)
                chunk(1, 0)
                fill(1)
                chunk(2, 0)
                fill(1)
                pe.wait_ge(lora_in, 32 * u + 32)
                after(V, "sk")
                mm(ps[:, 0, 0:T], w2s[:], tlw[:])
                E.step("lora", mm(ps[:, 0, T:2 * T], a2s[:], tla[:]))
                chunk(3, 0)
                fill(1)
                chunk(1, 1)
                fill(1)
                chunk(2, 1)
                fill(1)
                chunk(3, 1)
                fill(1)
                chunk(1, 2)
                after(V, "silu")
                after(A, "sqq")
                for t in range(NT):
                    o = ps[:, 1, 8 * t:8 * t + 8]
                    mm(o[:, 0:2], sq[:, 0, cols(t)], headsel[:])
                    mm(o[:, 2:3], sq[:, 1, cols(t)], ones[:])
                    mm(o[:, 3:4], sq[:, 2, cols(t)], ones[:])
                    last = mm(o[:, 4:6], prod[:, cols(t)], headsel[:])
                E.step("norms", last)
                chunk(2, 2)
                fill(1)
                chunk(3, 2)
                after(V, "rkx")
                after(G, "ub")
                for t in range(NT):
                    mm(ps[:, 3, cols(t)], ub[:, t, 1:2].to_broadcast([P, P]), cum_up)
                    mm(ps[:, 3, T + 2 * t:T + 2 * t + 1], cum_up, ub[:, t, 1:2])
                    mm(ps[:, 3, T + 2 * t + 1:T + 2 * t + 2], strict_lo[:], ub[:, t, 1:2])
                    mm(ps[:, 2, cols(t)], rn[:, t, 2:3].to_broadcast([P, P]), ident[:])
                    mm(ps[:, 2, T + t * P:T + (t + 1) * P], rn[:, t, 3:4].to_broadcast([P, P]), ident[:])
                    mm(ps[:, 0, cols(t)], rne[:, t, :], ident[:])
                    last = mm(ps[:, 0, T + t * P:T + (t + 1) * P], ub[:, t, 0:1].to_broadcast([P, P]), ident[:])
                E.step("rows", last)
                chunk(1, 3)
                fill(1)
                chunk(2, 3)
                fill(1)
                chunk(3, 3)
                fill(1)
                after(V, "qde")
                after(A, "ah1")
                for t in range(NT):
                    nc.tensor.transpose(ps[:, 1, cols(t)], rkv[:, 2, cols(t)], ident[:])
                    nc.tensor.transpose(ps[:, 1, T + t * P:T + (t + 1) * P], qkv[:, 2, cols(t)], ident[:])
                    nc.tensor.transpose(ps[:, 2, cols(t)], bhk[:, 0, cols(t)], ident[:])
                    nc.tensor.transpose(ps[:, 2, T + t * P:T + (t + 1) * P], bhk[:, 1, cols(t)], ident[:])
                    last = nc.tensor.transpose(ps[:, 0, cols(t)], kn[:, cols(t)], ident[:])
                E.step("tok", last)
                if prev:
                    gate_pe(pe, u, 1)
                for i, (bank, who, name) in enumerate(((3, None, None), (1, A, "vb1"), (2, A, "bk"), (0, A, "kd1"))):
                    if who is not None:
                        after(who, name)
                    t, h = i // 2, i % 2
                    mm(ps[:, bank, 0:2 * P], bhk[:, 0, cols(t)], arh[:, h, :, cols(t)])
                    E.step(f"in{i}", mm(ps[:, bank, 2 * P:4 * P], bhk[:, 1, cols(t)], arh[:, h, :, cols(t)]))
                fill(1)
                after(V, "t0")
                for i in range(4):
                    t, h = i // 2, i % 2
                    last = mm(ps[:, 3, i * P:(i + 1) * P], arh[:, h, 0, cols(t)], bhk[:, 0, cols(t)])
                E.step("nab", last)
                for t, bank in enumerate((1, 2)):
                    after(V, f"t{t + 1}")
                    mm(ps[:, bank, 0:2 * P], kn[:, cols(t)], kq[:, :, cols(t)])
                    E.step(f"g{t}", mm(ps[:, bank, 2 * P:3 * P], kq[:, 0, cols(t)], kn[:, cols(t)]))
                fill(2)
                for i in LV:
                    m = 2 << i
                    after(V, f"x{i - 1}" if i else "xi")
                    for p in range(6):
                        lt = tr[:, p, 0, :] if p < 4 else tg[:, p - 4, 0, :]
                        last = mm(ps[:, 2 + i % 2, 64 * p:64 * p + 64], lt, half1(xi[:, p, :], m, 0))
                    E.step(f"Y{i}", last)
                    fill(1)
                    if i == 0:
                        after(G, "xti")
                    after(V, f"y{i}")
                    for p in range(6):
                        if i < 4:
                            mm(ps[:, 0, 64 * p:64 * p + 64], xt_[:, p, :], half1(yb[i % 2][:, p, :], m, 0))
                        last = mm(ps[:, 1, 64 * p:64 * p + 64], yb[i % 2][:, p, :], half1(xt_[:, p, :], m, 1))
                    E.step(f"X{i}", last)
                    fill(1)
                    if i == 3 and prev:
                        turn_pe(pe, u, 1)
                fill(1)
                assert not more or q_at[0] == FIRST + QU, q_at[0]

            def finish_pe(pe, u):
                wait(pe, AB, "mT", u, 1)
                for c in CN:
                    for k in (1, 2, 3):
                        chunk_pe(pe, u, 0, k, c)
                gate_pe(pe, u, 0)
                turn_pe(pe, u, 0)

            def chunk_act(act, u, lag, k, c):
                t, b = c // 2, c % 2
                rb = slice(CH * b, CH * b + CH)

                def fn(name, o, i, **kw):
                    AB.step(name, nc.scalar.activation(o, i, ACT.Copy, **kw))

                wait(act, EB, f"c{(1, 2, 4)[k - 1]}_{c}", u, lag)
                if k == 1:
                    fn(f"r{c}", rhs[:, 0, :], ps[:, 4, 0:P])
                elif k == 2:
                    fn(f"un{c}", un[b][rb, :], ps[rb, 4, P:2 * P], scale=-1.0)
                else:
                    fn(f"y{c}", yy[rb, t, :], ps[rb, 4, 2 * P:3 * P])
                    fn(f"o{c}", oo[rb, t, :], ps[rb, 4, 3 * P:4 * P])

            def squares_act(act, u, lag):
                wait(act, VB, "yc", u, lag)
                AB.step("ysq", nc.scalar.activation(sqo[:, 0, :], yy[:].rearrange("p a b -> p (a b)"), ACT.Square))
                wait(act, AB, "o3", u, lag)
                AB.step("osq", nc.scalar.activation(sqo[:, 1, :], oo[:].rearrange("p a b -> p (a b)"), ACT.Square))

            def turn_act(act, u, lag):
                wait(act, EB, "mT", u, lag)
                at = bass.ds(u - lag, 1)
                AB.step("mT", nc.scalar.activation(mixT[:, at, :], ps[:, 4:5, 0:T], ACT.Copy))

            def mix_act(act, u, prev, more):
                q_at = [FIRST + LEAD]

                def fill(n):
                    for _ in range(n):
                        if more or q_at[0] < QU:
                            split_hi(act, u, q_at[0])
                            q_at[0] += 1

                def chunk(k, c):
                    if prev:
                        chunk_act(act, u, 1, k, c)

                def after(steps, name):
                    wait(act, steps, name, u)

                def fn(name, o, i, f=ACT.Copy, **kw):
                    A.step(name, nc.scalar.activation(o, i, f, **kw))

                fill(1)
                after(E, "tr1")
                after(G, "up")
                for i, x in enumerate("rkv"):
                    fn(f"u{x}", rkv[:, i, :], ps[:, i // 2, (i % 2) * T:(i % 2 + 1) * T],
                       scale=up[:, OMM + i:OMM + i + 1])
                chunk(1, 0)
                after(E, "tr2")
                for i, x in enumerate("qkv"):
                    fn(f"c{x}", qkv[:, i, :], ps[:, 2 + i // 2, (i % 2) * T:(i % 2 + 1) * T],
                       scale=up[:, TAP[3] + i:TAP[3] + i + 1])
                fill(1)
                chunk(2, 0)
                fill(1)
                after(E, "lora")
                fn("tw", sig[:], ps[:, 0, 0:T], ACT.Tanh, scale=0.5, bias=up[:, HW0:HW0 + 1])
                fn("ta", al[:], ps[:, 0, T:2 * T], ACT.Tanh, scale=0.5, bias=up[:, HA0:HA0 + 1])
                if more:
                    load_lora(act, u + 1)
                fill(1)
                chunk(3, 0)
                chunk(1, 1)
                after(V, "kx")
                fn("sqk", sq[:, 0, :], kk[:], ACT.Square)
                fn("tq", th[:].rearrange("p (a b) -> p a b", a=3), qkv[:], ACT.Tanh, scale=0.5)
                fill(1)
                chunk(2, 1)
                after(V, "cex")
                fn("wex", wex[:], wex[:], ACT.Exp, scale=-KAPPA)
                fn("winv", winv[:], cum[:], ACT.Exp, scale=KAPPA)
                fn("winc", winc[:], cum[:], ACT.Exp, scale=-KAPPA)
                chunk(3, 1)
                fill(1)
                after(V, "silu")
                fn("sqq", sq[:, 1:3, :], qkv[:, 0:2, :], ACT.Square)
                chunk(1, 2)
                take_out(act, u, 2)
                fill(1)
                chunk(2, 2)
                chunk(3, 2)
                after(E, "rows")
                fn("egr", egr[:], ps[:, 3, 0:T], ACT.Exp)
                fn("ege", ege[:].rearrange("p a b -> p (a b)"), ps[:, 3, T:T + 4], ACT.Exp)
                fill(1)
                chunk(1, 3)
                after(V, "dl1")
                fn("edt", dd[:, :, 0, :], dd[:, :, 0, :], ACT.Exp)
                fn("edl", dd[:, :, 1, :], dd[:, :, 1, :], ACT.Exp, scale=-1.0)
                chunk(2, 3)
                fill(1)
                chunk(3, 3)
                fill(1)
                after(V, "rr")
                for h in range(2):
                    hp = slice(RH * h, RH * h + RH)
                    fn(f"ah{h}", arh[hp, h, :, :], ar[hp, :, :])
                fill(1)
                after(E, "tok")
                after(G, "uh")
                fn("v", vt.rearrange("p a b -> p (a b)"), ps[:, 1, 0:T])
                for t in range(NT):
                    fn(f"vb{t}", vb[:, t, :], ps[:, 1, T + t * P:T + (t + 1) * P], scale=uh[:, t:t + 1])
                fn("bk", bkt[:].rearrange("p a t b -> p (a t b)"), ps[:, 2, :])
                for t in range(NT):
                    fn(f"kd{t}", kd[:, t, :], ps[:, 0, cols(t)], scale=ege[:, t, 1:2])
                fn("gates", thg, pu[:, :, 2 * PW:3 * PW], ACT.Tanh, scale=0.5)
                if prev:
                    wait(act, EB, "gate", u, 1)
                    load_gate(act, u)
                fill(2)
                if prev:
                    after(G, "dml")
                    squares_act(act, u, 1)
                for i in LV:
                    fill(2)
                    if i == 0 and more:
                        take_out(act, u, 3)
                    if i == 3 and prev:
                        turn_act(act, u, 1)
                        load_lnw(act, u)
                    if i == 4 and more:
                        take_out(act, u, 4)
                fill(1)
                if more:
                    after(G, "bvb")
                    load_lnb(act, u + 1)
                assert not more or q_at[0] == FIRST + QU + LEAD, q_at[0]

            def finish_act(act, u):
                for c in CN:
                    for k in (1, 2, 3):
                        chunk_act(act, u, 0, k, c)
                squares_act(act, u, 0)
                turn_act(act, u, 0)

            def tt_v(steps, name, o, x, y, op=ALU.mult):
                steps.step(name, nc.vector.tensor_tensor(o, x, y, op))

            def ts_v(steps, name, o, x, s1, s2, op0, op1=ALU.bypass):
                if s2 is None:
                    steps.step(name, nc.vector.tensor_scalar(o, x, s1, None, op0))
                else:
                    steps.step(name, nc.vector.tensor_scalar(o, x, s1, s2, op0, op1))

            def stv_v(steps, name, o, x, s, y, op0=ALU.mult, op1=ALU.add):
                steps.step(name, nc.vector.scalar_tensor_tensor(o, x, s, y, op0, op1))

            def chunk_dve(dve, u, lag, k, c):
                t, b = c // 2, c % 2
                rb = slice(CH * b, CH * b + CH)

                def after(steps, name):
                    wait(dve, steps, name, u, lag)

                if k == 1:
                    if c > 0:
                        after(EB, f"c1_{c}")
                        stv_v(VB, f"g{c}c", rhs[:, 1, :], ps[:, 5, 0:P], nege[:, t:t + 1], vb[:, t, :])
                        if c < 3:
                            after(VB, f"s{c - 1}b")
                            ts_v(VB, f"sw{c}", stw[:], st[:], wlast[:, c:c + 1], None, ALU.mult)
                elif k == 2:
                    after(EB, f"c2_{c}")
                    VB.step(f"vn{c}", nc.vector.tensor_copy(vn[b][rb, :], ps[rb, 5, P:2 * P]))
                elif c < 3:
                    if c > 0:
                        after(EB, f"c4_{c}")
                        after(VB, f"sw{c}")
                    else:
                        after(EB, "c3_0")
                    for h in range(2):
                        hp = slice(RH * h, RH * h + RH)
                        o = ps[hp, 5, 2 * P + RH * h:2 * P + RH * h + RH]
                        if c == 0:
                            ts_v(VB, f"s0{'ab'[h]}", st[hp, hp], o, wlast[hp, c:c + 1], None, ALU.mult)
                        else:
                            stv_v(VB, f"s{c}{'ab'[h]}", st[hp, hp], o, wlast[hp, c:c + 1], stw[hp, hp])
                    if c == 0:
                        VB.step("sg0", nc.vector.tensor_copy(sg[:], ps[:, 5, 3 * P:4 * P]))
                    else:
                        stv_v(VB, f"sg{c}", sg[:], sg[:], glast[:, c:c + 1], ps[:, 5, 3 * P:4 * P])

            def output_dve(dve, u, lag, part):
                def after(steps, name):
                    wait(dve, steps, name, u, lag)

                def done(name):
                    after(VB, name)

                def tt(*x):
                    tt_v(VB, *x)

                y4 = yy[:].rearrange("p t (h j) -> p (t h) j", h=2)
                if part == 0:
                    after(AB, "o3")
                    VB.step("ys", nc.vector.tensor_reduce(ym[:], y4, AX.X, ALU.add))
                    done("ys")
                    ts_v(VB, "nm", ym[:], ym[:], 1.0 / RH, None, ALU.mult)
                    done("nm")
                    tt("yc", y4, y4, ym[:].unsqueeze(2).to_broadcast([P, 4, RH]), ALU.subtract)
                elif part == 1:
                    after(AB, "osq")
                    VB.step("yv", nc.vector.tensor_reduce(
                        stt[:, 0:4], sqo[:, 0, :].rearrange("p (a j) -> p a j", j=RH), AX.X, ALU.add))
                    VB.step("ov", nc.vector.tensor_reduce(
                        stt[:, 4:6], sqo[:, 1, :].rearrange("p (a j) -> p a j", j=P), AX.X, ALU.add))
                    done("ov")
                    tt("st1", stt[:], stt[:], st_scale[:])
                    done("st1")
                    tt("st2", stt[:], stt[:], st_eps[:], ALU.add)
                    done("st2")
                    rsqrt(nc, dve, VB, "r", u, rs[:], stt[:], rst[:], lag)
                    tt("yn", y4, y4, rs[:, 0:4].unsqueeze(2).to_broadcast([P, 4, RH]))
                elif part == 2:
                    dve.wait_ge(lnw_in, 16 * u + (16 - 16 * lag))
                    done("yn")
                    tt("ylw", yy[:], yy[:], lnw[:].unsqueeze(1).to_broadcast([P, NT, P]))
                    after(G, "bvb")
                    done("ylw")
                    tt("ybv", yy[:], yy[:], bv[:], ALU.add)
                    after(EB, "gate")
                    done("ybv")
                    tt("yg", yy[:], yy[:], ps[:, 5, 0:T].rearrange("p (a b) -> p a b", a=NT))
                    done("yg")
                    tt("yga", yy[:], yy[:], ga[:])
                else:
                    after(GB, "ogb")
                    done("yga")
                    tt("mix", yy[:], yy[:], oo[:], ALU.add)

            def mix_dve(dve, u, prev, more):
                q_at = [FIRST + LEAD]

                def fill(n):
                    for _ in range(n):
                        if more or q_at[0] < QU:
                            split_lo(dve, u, q_at[0])
                            q_at[0] += 1

                def chunk(k, c):
                    if prev:
                        chunk_dve(dve, u, 1, k, c)

                def output(part):
                    if prev:
                        output_dve(dve, u, 1, part)

                def after(steps, name):
                    wait(dve, steps, name, u)

                def done(name):
                    after(V, name)

                def tt(*x):
                    tt_v(V, *x)

                def ts(*x):
                    ts_v(V, *x)

                def stv(*x):
                    stv_v(V, *x)

                fill(1)
                after(A, "uv")
                for i, x in enumerate("rkv"):
                    stv(f"s{x}", rkv[:, i, 1:T], ps[:, i // 2, (i % 2) * T:(i % 2 + 1) * T - 1],
                        up[:, MIX_R + i:MIX_R + i + 1], rkv[:, i, 1:T])
                chunk(2, 0)
                after(A, "cv")
                for j in range(3):
                    d = 3 - j
                    for i, x in enumerate("qkv"):
                        if j:
                            done(f"c{j - 1}{x}")
                        stv(f"c{j}{x}", qkv[:, i, d:T], ps[:, 2 + i // 2, (i % 2) * T:(i % 2 + 1) * T - d],
                            up[:, TAP[j] + i:TAP[j] + i + 1], qkv[:, i, d:T])
                    if j == 0:
                        fill(1)
                    elif j == 1:
                        chunk(3, 0)
                done("sv")
                ts("kx", kk[:], rkv[:, 1, :], up[:, K_K:K_K + 1], None, ALU.mult)
                fill(1)
                chunk(1, 1)
                after(A, "ta")
                ts("sig", sig[:], sig[:], 0.5, 0.5, ALU.mult, ALU.add)
                ts("al", al[:], al[:], 0.5, 0.5, ALU.mult, ALU.add)
                done("sig")
                V.step("cum", nc.vector.tensor_tensor_scan(cum[:], restart[:], sig[:], 0.0, ALU.mult, ALU.add))
                done("cum")
                tt("cex", wex[:], cum[:], sig[:], ALU.subtract)
                fill(1)
                chunk(2, 1)
                fill(1)
                ts("kf", kmod[:], al[:], up[:, K_A:K_A + 1], up[:, OKA:OKA + 1], ALU.mult, ALU.add)
                done("kf")
                tt("kmod", kmod[:], kmod[:], rkv[:, 1, :])
                ts("rr0", prod[:], rkv[:, 0, :], up[:, R_K:R_K + 1], None, ALU.mult)
                done("rr0")
                tt("pr", prod[:], prod[:], kmod[:])
                chunk(3, 1)
                fill(1)
                after(A, "tq")
                stv("silu", qkv[:], th[:].rearrange("p (a b) -> p a b", a=3), 1.0, qkv[:], ALU.add, ALU.mult)
                chunk(1, 2)
                fill(1)
                after(E, "norms")
                sums = ps[:, 1, 0:16].rearrange("p (t c) -> p t c", t=NT)
                tt("nrm", nrm[:], sums[:, :, 0:4], eps4[:].unsqueeze(1).to_broadcast([P, NT, 4]), ALU.add)
                V.step("bon", nc.vector.tensor_copy(bon[:], sums[:, :, 4:6]))
                chunk(2, 2)
                done("nrm")
                rsqrt(nc, dve, V, "n", u, rn[:], nrm[:], rtmp[:])
                ts("rq", rn[:, :, 2:3], rn[:, :, 2:3], P ** -0.5, None, ALU.mult)
                V.step("rkx", nc.vector.tensor_copy(rne.rearrange("p t (h j) -> p t h j", h=2),
                                                    rn[:, :, 0:2].unsqueeze(3).to_broadcast([P, NT, 2, RH])))
                chunk(3, 2)
                fill(1)
                after(A, "ege")
                V.step("gcc", nc.vector.tensor_copy(gcc[:], ps[:, 3, T:T + 4:2]))
                done("gcc")
                for t in range(NT):
                    ts(f"dt{t}", dd[:, t, 0, :], ps[:, 3, cols(t)], gcc[:, t:t + 1], 0.0, ALU.subtract, ALU.min)
                    ts(f"dl{t}", dd[:, t, 1, :], ps[:, 3, cols(t)], gcc[:, t:t + 1], 0.0, ALU.subtract, ALU.max)
                chunk(1, 3)
                fill(1)
                tt("kk", kk[:], kk[:], ps[:, 0, 0:T])
                tt("kn", kn[:], qkv[:, 1, :], ps[:, 2, T:2 * T])
                tt("qn", kq[:, 1, :], qkv[:, 0, :], ps[:, 2, 0:T])
                after(A, "winc")
                tt("aw", al[:], al[:], winv[:])
                tt("kh", bhk[:, 1, :], kmod[:], winv[:])
                chunk(2, 3)
                fill(1)
                if prev:
                    wait(dve, EB, "c4_3", u, 1)
                ts("nege", nege[:], ege[:, :, 0], -1.0, None, ALU.mult)
                ts("wlast", wlast[:], winc[:, CH - 1:T:CH], 1.0, None, ALU.mult)
                ts("glast", glast[:], egr[:, CH - 1:T:CH], 1.0, None, ALU.mult)
                done("kn")
                tt("kb", kq[:, 0, :], kn[:], ps[:, 0, T:2 * T])
                done("kk")
                tt("ap", ar[:, 0, :], kk[:], wex[:])
                tt("rr", ar[:, 1, :], rkv[:, 0, :], winc[:])
                done("aw")
                tt("bh", bhk[:, 0, :], al[:], kk[:])
                done("qn")
                tt("qde", qde[:], kq[:, 1, :], egr[:])
                fill(1)
                for i, bank in enumerate((3, 1, 2, 0)):
                    after(E, f"in{i}")
                    tt(f"t{i}", tr[:, i, :, :].rearrange("p (g a) b -> p g a b", g=2),
                       ps[:, bank, :].rearrange("p (g a b) -> p g a b", g=2, a=2),
                       up_masks[:].unsqueeze(1).to_broadcast([P, 2, 2, P]))
                after(E, "nab")
                tt("nab", xi[:, 0:4, :], ps[:, 3, :].rearrange("p (a b) -> p a b", a=4),
                   strict_lo[:].unsqueeze(1).to_broadcast([P, 4, P]))
                after(G, "dml")
                for t, bank in enumerate((1, 2)):
                    after(E, f"g{t}")
                    tt(f"g{t}", tg[:, t, :, :], ps[:, bank, 0:2 * P].rearrange("p (a b) -> p a b", a=2),
                       dm[:, t, 0:2, :])
                    tt(f"l{t}", xi[:, 4 + t, :], ps[:, bank, 2 * P:3 * P], dm[:, t, 2, :])
                fill(1)
                output(0)
                done("l1")
                tt("xm", xi[:], xi[:], lev[:, 0:1, :].to_broadcast([P, 6, P]))
                done("xm")
                tt("xi", xi[:], ident[:].unsqueeze(1).to_broadcast([P, 6, P]), xi[:], ALU.subtract)
                fill(1)
                for i in LV:
                    m = 2 << i
                    nb = P // (2 * m)

                    def compact(bank):
                        return ps[:, bank, 0:6 * 64].rearrange("p (a b j) -> p a b j", a=6, j=m)

                    after(E, f"Y{i}")
                    if i < 2:
                        after(G, "zb")
                    else:
                        after(G, f"z{i - 2}")
                    tt(f"y{i}", half(yb[i % 2][:], m, 0), compact(2 + i % 2),
                       half1(lev[:, i + 1, :], m, 0).unsqueeze(1).to_broadcast([P, 6, nb, m]))
                    fill(1)
                    after(E, f"X{i}")
                    if i < 4:
                        tt(f"x{i}", half(xi[:], m, 0), half(xi[:], m, 0), compact(0), ALU.subtract)
                    tt(f"xt{i}", half(xt_[:], m, 1), half(xt_[:], m, 1), compact(1), ALU.subtract)
                    fill(1)
                    if i < 3:
                        output(i + 1)
                fill(1)
                after(A, "gates")
                if prev:
                    wait(dve, VB, "mix", u, 1)
                ts("ga", ga[:], thg[:, :, P:2 * P], 0.5, 0.5, ALU.mult, ALU.add)
                stv("gz", gb[:], thg[:, :, 0:P], 1.0, pu[:, :, 2 * PW:2 * PW + P], ALU.add, ALU.mult)
                done("gz")
                stv("gb", gb[:], thg[:, :, 2 * P:3 * P], 1.0, gb[:], ALU.add, ALU.mult)
                assert not more or q_at[0] == FIRST + QU + LEAD, q_at[0]

            def finish_dve(dve, u):
                for c in CN:
                    for k in (1, 2, 3):
                        chunk_dve(dve, u, 0, k, c)
                for part in range(4):
                    output_dve(dve, u, 0, part)

            def tt_g(steps, name, o, x, y, op=ALU.mult):
                steps.step(name, nc.gpsimd.tensor_tensor(o, x, y, op))

            def output_pool(pool, u, lag):
                wait(pool, VB, "r10", u, lag)
                tt_g(GB, "on", oo[:], oo[:], rs[:, 4:6].unsqueeze(2).to_broadcast([P, NT, P]))
                wait(pool, GB, "on", u, lag)
                tt_g(GB, "onw", oo[:], oo[:], gnw[:].unsqueeze(1).to_broadcast([P, NT, P]))
                wait(pool, GB, "onw", u, lag)
                tt_g(GB, "ogb", oo[:], oo[:], gb[:])

            def mix_pool(pool, u, prev):
                def after(steps, name):
                    wait(pool, steps, name, u)

                def tt(*x):
                    tt_g(G, *x)

                def clear(name, tile):
                    eye = ident[:].unsqueeze(1).to_broadcast([P, 6, P])
                    tt(name, tile[:], eye, eye, ALU.subtract)

                if prev:
                    wait(pool, V, "xt4", u, 1)
                tt("up", up[:].unsqueeze(2), par[:, :, bass.ds(u, 1)], ones[:].unsqueeze(1).to_broadcast([P, NPAR, 1]))
                clear("za", yb[0])
                clear("zb", yb[1])
                for t in range(NT):
                    last = nc.gpsimd.tensor_tensor(ub[:, t, :].unsqueeze(2), bg[:, t, :, bass.ds(u, 1)],
                                                   ones[:].unsqueeze(1).to_broadcast([P, 2, 1]), ALU.mult)
                G.step("ub", last)
                after(G, "ub")
                tt("uh", uh[:], ub[:, :, 0], halves[:].to_broadcast([P, NT]))
                after(A, "edl")
                for t in range(NT):
                    tt(f"dm{t}", dm[:, t, 0:2, :], dd[:, t, 0:1, :].to_broadcast([P, 2, P]), up_masks[:])
                tt("dml", dm[:, :, 2, :], dd[:, :, 1, :], strict_lo[:].unsqueeze(1).to_broadcast([P, NT, P]))
                after(A, "v")
                for b in range(2):
                    rb = slice(CH * b, CH * b + CH)
                    after(G, ("dml", "vp0")[b])
                    tt(f"vp{b}", vp[b][rb, :, :], vt[rb, :, :], ones[rb, :].unsqueeze(1).to_broadcast([CH, NT, P]))
                after(V, "l1")
                lt1 = lev[:, 6:7, :]
                after(G, "vp1")
                tt("xtm", xt_[:, 0:4, :], tr[:, :, 0, :], lt1.to_broadcast([P, 4, P]))
                tt("xtg", xt_[:, 4:6, :], tg[:, :, 0, :], lt1.to_broadcast([P, 2, P]))
                after(G, "xtg")
                tt("xti", xt_[:], ident[:].unsqueeze(1).to_broadcast([P, 6, P]), xt_[:], ALU.subtract)
                after(E, "X0")
                clear("z0", yb[0])
                if prev:
                    output_pool(pool, u, 1)
                after(E, "X1")
                clear("z1", yb[1])
                after(E, "X2")
                clear("z2", yb[0])
                if prev:
                    wait(pool, VB, "ybv", u, 1)
                after(V, "bon")
                tt("bv", bv[:].rearrange("p t (h j) -> p t h j", h=2), vt.rearrange("p t (h j) -> p t h j", h=2),
                   bon[:].unsqueeze(3).to_broadcast([P, NT, 2, RH]))
                pool.wait_ge(lnb_in, 16 * u + 16)
                after(G, "bv")
                tt("bvb", bv[:], bv[:], lnb[:].unsqueeze(1).to_broadcast([P, NT, P]), ALU.add)

            with nc.Block() as block:
                @block.sync
                def _(sp):
                    load_unit_weights(sp, 0)
                    with sp.Fori(1, NU) as u:
                        load_unit_weights(sp, u)

                @block.gpsimd
                def _(pool):
                    for tile in (arh, vp[0], vp[1], un[0], un[1], vn[0], vn[1], st):
                        nc.gpsimd.memset(tile[:], 0.0)
                    mix_pool(pool, 0, False)
                    with pool.Fori(1, NU) as u:
                        mix_pool(pool, u, True)
                    output_pool(pool, NU - 1, 0)

                @block.scalar
                def _(act):
                    for q in range(FIRST + LEAD):
                        split_hi(act, 0, q)
                        if q % 8 == 1 and q > 8:
                            take_out(act, 0, q // 8 - 1)
                    mix_act(act, 0, False, True)
                    with act.Fori(1, NU - 1) as u:
                        mix_act(act, u, True, True)
                    mix_act(act, NU - 1, True, False)
                    finish_act(act, NU - 1)

                @block.vector
                def _(dve):
                    for q in range(FIRST + LEAD):
                        split_lo(dve, 0, q)
                    mix_dve(dve, 0, False, True)
                    with dve.Fori(1, NU - 1) as u:
                        mix_dve(dve, u, True, True)
                    mix_dve(dve, NU - 1, True, False)
                    finish_dve(dve, NU - 1)

                @block.tensor
                def _(pe):
                    for q in range(FIRST):
                        project(pe, 0, q)
                    mix_pe(pe, 0, False, True)
                    with pe.Fori(1, NU - 1) as u:
                        mix_pe(pe, u, True, True)
                    mix_pe(pe, NU - 1, True, False)
                    finish_pe(pe, NU - 1)
        mix_ctx.close()

        CB = 512
        NB = D // CB
        wr = sb("wr", [P, 4, 4, CB])
        whi = [sb(f"whi{i}", [P, 2, CB], F32R) for i in range(2)]
        wlo = [sb(f"wlo{i}", [P, 2, CB], F32R) for i in range(2)]
        row = sb("row", [P, D])
        ssy = sb("ssy", [P, NT, NB])
        ssx = sb("ssx", [P, NT])
        rr = sb("rr", [P, NT])
        rtm = sb("rtm", [P, NT])
        x2 = keep[:].rearrange("p a b -> p (a b)").rearrange("p (t n) -> p t n", t=NT)

        class Stream:

            def __init__(self, tag):
                self.landed = [sem(f"{tag}_in{i}") for i in range(4)]
                self.hi, self.lo, self.used = sem(f"{tag}_hi"), sem(f"{tag}_lo"), sem(f"{tag}_used")

        def stage_hi(act, s, n, src):
            if not (isinstance(n, int) and n < 2):
                act.wait_ge(s.used, n - 1)
            nc.scalar.activation(whi[s.par][:], src, ACT.Copy).then_inc(s.hi, 1)
            s.par ^= 1

        def stage_lo(dve, s, n, src):
            dve.wait_ge(s.hi, n + 1)
            nc.vector.tensor_tensor(wlo[s.par][:], src, whi[s.par][:].bitcast(F32), ALU.subtract).then_inc(s.lo, 1)
            s.par ^= 1

        def stage_mm(pe, s, n, left_hi, left_lo, o, first, last):
            pe.wait_ge(s.lo, n + 1)
            for k in range(2):
                for t in range(NT):
                    xs = slice(t * P, (t + 1) * P)
                    nc.tensor.matmul(o(t), left_hi[:, k, xs], whi[s.par][:, k, :], start=first and k == 0, stop=False,
                                     skip_group_check=True)
                    nc.tensor.matmul(o(t), left_hi[:, k, xs], wlo[s.par][:, k, :], start=False, stop=False,
                                     skip_group_check=True)
                    mm = nc.tensor.matmul(o(t), left_lo[:, k, xs], whi[s.par][:, k, :], start=False,
                                          stop=last and k == 1, skip_group_check=True)
            mm.then_inc(s.used, 1)
            s.par ^= 1

        post_act = [f"sq{i}" for i in range(2 * NB)]
        post_dve = ["sum", "var"] + rsqrt_names("p") + ["n0", "n1", "a0", "a1"]

        def post_norm_act(act, A, junk, used, n):
            act.wait_ge(used, n)
            for t in range(NT):
                for b in range(NB):
                    if t + b:
                        act.wait_ge(A.sem, A.after(f"sq{t * NB + b - 1}"))
                    A.step(f"sq{t * NB + b}", nc.scalar.activation(junk, ps[:, 2 * b + t, :], ACT.Square,
                                                                   accum_out=ssy[:, t, b:b + 1]))

        def post_norm_dve(dve, A, V, y, base, dst):
            def done(name):
                dve.wait_ge(V.sem, V.after(name))

            dve.wait_ge(A.sem, A.after(f"sq{2 * NB - 1}"))
            V.step("sum", nc.vector.tensor_reduce(ssx[:], ssy[:], AX.X, ALU.add))
            done("sum")
            V.step("var", nc.vector.tensor_scalar(ssx[:], ssx[:], 1.0 / D, NORM_EPS, ALU.mult, ALU.add))
            done("var")
            rsqrt(nc, dve, V, "p", 0, rr[:], ssx[:], rtm[:])
            for t in range(NT):
                banks = ps[:].rearrange("p (n t) c -> p n t c", t=NT)[:, :, t, :]
                V.step(f"n{t}", nc.vector.scalar_tensor_tensor(
                    y[:, t, :].rearrange("p (n c) -> p n c", c=CB), banks, rr[:, t:t + 1],
                    row[:].rearrange("p (n c) -> p n c", c=CB), ALU.mult, ALU.mult))
            for t in range(NT):
                done(f"n{t}")
                V.step(f"a{t}", nc.vector.tensor_tensor(dst[:, t, :], y[:, t, :], base[:, t, :], ALU.add))

        with ExitStack() as c3:
            x1 = sb("x1", [P, NT, D], F32, c3)
            y1 = sb("y1", [P, NT, D], F32, c3)
            junk = sb("junk3", [P, D], F32, c3)
            S = Stream("out")
            x1_in, row_in = sem("x1_in"), sem("row_in")
            A = Steps(sem("out_act"), ["xh"] + post_act + ["ss0", "ss1", "xs0", "xs1"] + [f"hi{g}" for g in G8])
            V = Steps(sem("out_dve"), ["xl"] + post_dve + ["v2"] + rsqrt_names("q") + [f"lo{g}" for g in G8])
            E = Steps(sem("out_pe"), [f"x{g}" for g in G8])
            w3 = a["w_out"][0].rearrange("(kc p) n -> p kc n", p=P)
            QB = KC // 2

            def quantum(q):
                return wr[:, (q // 2) % 4, 2 * (q % 2):2 * (q % 2) + 2, :]

            with nc.Block() as block:
                @block.sync
                def _(sp):
                    def load(b, i):
                        sp.dma_start(wr[:, i, :, :], w3[:, 4 * i:4 * i + 4, bass.ds(b * CB, CB)]
                                     ).then_inc(S.landed[i], 16)

                    for i in range(4):
                        load(0, i)
                    sp.dma_start(x1[:], a["x"][0].rearrange("(t p) n -> p t n", p=P)).then_inc(x1_in, 16)
                    sp.dma_start(row[:], a["norm_mix_post"][0].partition_broadcast(P)).then_inc(row_in, 16)
                    with sp.Fori(1, NB) as b:
                        for i in range(4):
                            sp.wait_ge(S.lo, b * QB + 2 * i + 2 - QB)
                            load(b, i)

                @block.scalar
                def _(act):
                    S.par = 0
                    A.step("xh", nc.scalar.activation(xh[:], keep[:], ACT.Copy))

                    def block_hi(b):
                        for q in range(QB):
                            if q % 2 == 0:
                                act.wait_ge(S.landed[q // 2], b * 16 + 16)
                            stage_hi(act, S, b * QB + q, quantum(q))

                    block_hi(0)
                    with act.Fori(1, NB) as b:
                        block_hi(b)
                    post_norm_act(act, A, junk[:, 0:CB], S.used, NB * QB)
                    for t in range(NT):
                        act.wait_ge(V.sem, V.after(f"a{t}"))
                        if t:
                            act.wait_ge(A.sem, A.after("ss0"))
                        A.step(f"ss{t}", nc.scalar.activation(junk[:], x2[:, t, :], ACT.Square,
                                                              accum_out=ssx[:, t:t + 1]))
                    act.wait_ge(V.sem, V.after("q10"))
                    for t in range(NT):
                        A.step(f"xs{t}", nc.scalar.activation(y1[:, t, :], x2[:, t, :], ACT.Copy,
                                                              scale=rr[:, t:t + 1]))
                    transpose_x_act(act, A, E, NORM2)

                @block.vector
                def _(dve):
                    S.par = 0
                    dve.wait_ge(A.sem, A.after("xh"))
                    V.step("xl", nc.vector.tensor_tensor(xl[:], keep[:], xh[:].bitcast(F32), ALU.subtract))

                    def block_lo(b):
                        for q in range(QB):
                            stage_lo(dve, S, b * QB + q, quantum(q))

                    with dve.Fori(0, NB) as b:
                        block_lo(b)
                    dve.wait_ge(x1_in, 16)
                    dve.wait_ge(row_in, 16)
                    post_norm_dve(dve, A, V, y1[:], x1[:], x2)
                    dve.wait_ge(A.sem, A.after("ss1"))
                    V.step("v2", nc.vector.tensor_scalar(ssx[:], ssx[:], 1.0 / D, NORM_EPS, ALU.mult, ALU.add))
                    dve.wait_ge(V.sem, V.after("v2"))
                    rsqrt(nc, dve, V, "q", 0, rr[:], ssx[:], rtm[:])
                    transpose_x_dve(dve, V, A, NORM2)

                @block.tensor
                def _(pe):
                    S.par = 0
                    pe.wait_ge(V.sem, V.after("xl"))
                    with pe.Fori(0, NB) as b:
                        for q in range(QB):
                            stage_mm(pe, S, b * QB + q, xh[:, 2 * q:2 * q + 2, :], xl[:, 2 * q:2 * q + 2, :],
                                     lambda t: ps[:, bass.ds(b * NT + t, 1), :], q == 0, q == QB - 1)
                    pe.wait_ge(A.sem, A.after("xs1"))
                    transpose_x_pe(pe, E, y1, V)

        hidT = sb("hidT", [P, FKC, T])
        hh = [sb(f"hh{i}", [P, 2, T], F32R) for i in range(2)]
        hl = [sb(f"hl{i}", [P, 2, T], F32R) for i in range(2)]
        tg_ = sb("ffn_tanh", [P, NT, CB])
        gg = sb("ffn_gate", [P, NT, CB])
        hid = sb("ffn_hidden", [P, NT, CB])
        y2 = sb("y2", [P, NT, D])
        S = Stream("ffn")
        row2_in, result_out = sem("row2_in"), sem("result_out")
        tanh_done, gate_done, hidden_done = sem("tanh_done"), sem("gate_done"), sem("hidden_done")
        turned, stored = sem("turned"), sem("stored")
        down_in = [sem(f"down_in{i}") for i in range(2)]
        left_hi, left_lo = sem("left_hi"), sem("left_lo")
        A = Steps(sem("ffn_act"), post_act)
        V = Steps(sem("ffn_dve"), post_dve)
        wg = a["ffn_w_gate"][0].rearrange("(kc p) n -> p kc n", p=P)
        wu = a["ffn_w_up"][0].rearrange("(kc p) n -> p kc n", p=P)
        wd = a["ffn_w_down"][0].rearrange("(j k p) n -> j p k n", k=2, p=P)
        QF = 2 * (KC // 2)
        QD = QF * FB
        JD = FKC // 2

        def quantum(q):
            return wr[:, (q // 2) % 4, 2 * (q % 2):2 * (q % 2) + 2, :]

        def down_quantum(s, b):
            return wr[:, 2 * s:2 * s + 2, :, :].rearrange("p k a c -> p k (a c)")[:, :, b * CB:(b + 1) * CB]

        with nc.Block() as block:
            @block.sync
            def _(sp):
                def load(jb, f, first):
                    if not (first and f < 4):
                        sp.wait_ge(S.lo, jb * QF + 2 * f - 6)
                    w = wg if f < 4 else wu
                    kc = 4 * (f % 4)
                    sp.dma_start(wr[:, f % 4, :, :], w[:, kc:kc + 4, bass.ds(jb * CB, CB)]
                                 ).then_inc(S.landed[f % 4], 16)

                for f in range(8):
                    load(0, f, True)
                sp.dma_start(row[:], a["norm_ffn_post"][0].partition_broadcast(P)).then_inc(row2_in, 16)
                with sp.Fori(1, FB) as jb:
                    for f in range(8):
                        load(jb, f, False)

                def load_down(j, s, split):
                    sp.wait_ge(S.lo, split)
                    src = wd[j] if isinstance(j, int) else wd[bass.ds(j, 1)].rearrange("o p k n -> p (o k) n")
                    sp.dma_start(wr[:, 2 * s:2 * s + 2, :, :].rearrange("p k a c -> p k (a c)"), src
                                 ).then_inc(down_in[s], 16)

                load_down(0, 0, QD - 4)
                load_down(1, 1, QD)
                with sp.Fori(1, JD // 2) as jj:
                    for s in range(2):
                        load_down(jj * 2 + s, s, jj * (2 * NB) + (QD + (s + 1) * NB - 2 * NB))
                sp.wait_ge(V.sem, V.after("a1"))
                sp.dma_start(out[0].rearrange("(t p) n -> p t n", p=P), y2[:]).then_inc(result_out, 16)
                sp.wait_ge(result_out, 16)

            @block.scalar
            def _(act):
                S.par = 0

                def store(jb):
                    act.wait_ge(turned, jb + 1)
                    nc.scalar.activation(hidT[:, bass.ds(jb * 4, 4), :],
                                         ps[:, 4:6, :].rearrange("p a (k c) -> p (a k) c", c=T), ACT.Copy
                                         ).then_inc(stored, 1)

                def block_act(jb, first):
                    for q in range(QF):
                        if q % 2 == 0:
                            act.wait_ge(S.landed[(q // 2) % 4], jb * 32 + 16 * (q // 8 + 1))
                        stage_hi(act, S, jb * QF + q, quantum(q))
                        if q == 3 and not first:
                            store(jb - 1)
                        if q == 9:
                            act.wait_ge(S.used, jb * QF + QF // 2)
                            nc.scalar.activation(tg_[:], ps[:, 0:2, :], ACT.Tanh, scale=0.5).then_inc(tanh_done, 1)

                block_act(0, True)
                with act.Fori(1, FB) as jb:
                    block_act(jb, False)
                store(FB - 1)

                def down_act(j, s, n, landed):
                    if not isinstance(j, int):
                        act.wait_ge(S.used, n - NB)
                    nc.scalar.activation(hh[s][:], hidT[:, bass.ds(j * 2, 2), :], ACT.Copy).then_inc(left_hi, 1)
                    act.wait_ge(down_in[s], landed)
                    for b in range(NB):
                        stage_hi(act, S, n + b, down_quantum(s, b))

                act.wait_ge(stored, FB)
                for s in range(2):
                    down_act(s, s, QD + NB * s, 16)
                with act.Fori(1, JD // 2) as jj:
                    for s in range(2):
                        down_act(jj * 2 + s, s, jj * (2 * NB) + (QD + NB * s), jj * 16 + 16)
                post_norm_act(act, A, tg_[:, 0, :], S.used, QD + NB * JD)

            @block.vector
            def _(dve):
                S.par = 0

                def hidden(jb):
                    dve.wait_ge(S.used, jb * QF + QF)
                    nc.vector.scalar_tensor_tensor(hid[:], gg[:], 0.5, ps[:, 2:4, :], ALU.mult, ALU.mult
                                                   ).then_inc(hidden_done, 1)

                def block_dve(jb, first):
                    for q in range(QF):
                        stage_lo(dve, S, jb * QF + q, quantum(q))
                        if q == 1 and not first:
                            dve.wait_ge(gate_done, jb)
                            hidden(jb - 1)
                        if q == 9:
                            dve.wait_ge(tanh_done, jb + 1)
                            nc.vector.scalar_tensor_tensor(gg[:], tg_[:], 1.0, ps[:, 0:2, :], ALU.add, ALU.mult
                                                           ).then_inc(gate_done, 1)

                block_dve(0, True)
                with dve.Fori(1, FB) as jb:
                    block_dve(jb, False)
                dve.wait_ge(gate_done, FB)
                hidden(FB - 1)

                def down_dve(j, s, n):
                    dve.wait_ge(left_hi, j + 1)
                    nc.vector.tensor_tensor(hl[s][:], hidT[:, bass.ds(j * 2, 2), :], hh[s][:].bitcast(F32),
                                            ALU.subtract).then_inc(left_lo, 1)
                    for b in range(NB):
                        stage_lo(dve, S, n + b, down_quantum(s, b))

                for s in range(2):
                    down_dve(s, s, QD + NB * s)
                with dve.Fori(1, JD // 2) as jj:
                    for s in range(2):
                        down_dve(jj * 2 + s, s, jj * (2 * NB) + (QD + NB * s))
                dve.wait_ge(row2_in, 16)
                post_norm_dve(dve, A, V, y2[:], x2, y2[:])

            @block.tensor
            def _(pe):
                S.par = 0

                def turn(jb):
                    pe.wait_ge(hidden_done, jb + 1)
                    for k in range(4):
                        for t in range(NT):
                            c0 = (k % 2) * T + t * P
                            last = nc.tensor.transpose(ps[:, 4 + k // 2, c0:c0 + P], hid[:, t, k * P:(k + 1) * P],
                                                       ident[:])
                    last.then_inc(turned, 1)

                def block_pe(jb, first):
                    for q in range(QF):
                        g = q // (QF // 2)
                        if q == 0 and not first:
                            pe.wait_ge(gate_done, jb)
                        if q == 2 and not first:
                            turn(jb - 1)
                        kc = 2 * (q % (QF // 2))
                        stage_mm(pe, S, jb * QF + q, xh[:, kc:kc + 2, :], xl[:, kc:kc + 2, :],
                                 lambda t: ps[:, 2 * g + t, :], kc == 0, kc == KC - 2)

                block_pe(0, True)
                with pe.Fori(1, FB) as jb:
                    block_pe(jb, False)
                turn(FB - 1)
                pe.wait_ge(stored, FB)

                def down_pe(j, s, n, first, last):
                    pe.wait_ge(left_lo, j + 1)
                    for b in range(NB):
                        stage_mm(pe, S, n + b, hh[s][:], hl[s][:], lambda t: ps[:, 2 * b + t, :], first, last)

                for s in range(2):
                    down_pe(s, s, QD + NB * s, s == 0, False)
                with pe.Fori(1, JD // 2) as jj:
                    for s in range(2):
                        down_pe(jj * 2 + s, s, jj * (2 * NB) + (QD + NB * s), False, False)


_INS = ["x", "norm_mix_pre", "norm_mix_post", "norm_ffn_pre", "norm_ffn_post", "w_in", "rwkv_mix", "rwkv_w0",
        "rwkv_w2", "rwkv_a0", "rwkv_a2", "rwkv_g2", "rwkv_k_k", "rwkv_k_a", "rwkv_r_k", "rwkv_ln_w", "rwkv_ln_b",
        "gdn_conv_w", "gdn_a_log", "gdn_dt_bias", "gdn_norm_w", "w_out", "ffn_w_gate", "ffn_w_up", "ffn_w_down"]


def kernel(**inputs):
    import concourse.bacc as bacc
    from concourse.bass_utils import run_bass_kernel_spmd

    nc = bacc.Bacc("TRN2", target_bir_lowering=False, num_devices=1)
    arrays, aps = {}, {}
    for name in _INS:
        v = np.ascontiguousarray(inputs[name])
        arrays[f"in_{name}"] = v
        aps[name] = nc.dram_tensor(f"in_{name}", v.shape, mybir.dt.from_np(v.dtype), kind="ExternalInput").ap()
    out = nc.dram_tensor("out_x", (1, T, D), F32, kind="ExternalOutput").ap()
    build(nc, aps, out)
    r = run_bass_kernel_spmd(nc, [arrays], core_ids=[0])
    return r.results[0]["out_x"]
```
